# Optimizing a Trainium2 kernel written in Bass

```python
import math
import jax, jax.numpy as jnp
from jax import lax
import numpy as np

D_MODEL = 2048
BATCH = 1
SEQ = 256
DEPTH = 1

MOBA_HEADS = 8
MOBA_HEAD_DIM = 128
MOBA_WIDTH = MOBA_HEADS * MOBA_HEAD_DIM
MOBA_BLOCK = 256
MOBA_TOPK = 3
MOBA_Q_CHUNK = 64
PARTIAL_ROPE_DIM = MOBA_HEAD_DIM // 4
MLA_HEADS = 8
MLA_NOPE_DIM = 128
MLA_ROPE_DIM = 64
MLA_V_DIM = 128
MLA_Q_RANK = 512
MLA_KV_RANK = 256
MLA_WIDTH = MLA_HEADS * MLA_V_DIM
MLA_Q_BLOCK = 128
ROPE_THETA = 500000.0
D_FF = -(-8 * D_MODEL // (3 * 256)) * 256
EPS = 1e-6
N_BRANCHES = 2
IN_SIZES = (MOBA_WIDTH, MOBA_WIDTH, MOBA_WIDTH, MLA_Q_RANK, MLA_KV_RANK, MLA_ROPE_DIM, N_BRANCHES * D_MODEL)
IN_COLS = sum(IN_SIZES)


def rmsnorm(x, g):
    x32 = x.astype(jnp.float32)
    y = x32 * lax.rsqrt(jnp.mean(x32 * x32, axis=-1, keepdims=True) + EPS)
    return (y * g.astype(jnp.float32)).astype(x.dtype)

def rope(x, positions):
    d = x.shape[-1]
    inv_freq = ROPE_THETA ** (-jnp.arange(0, d, 2, dtype=jnp.float32) / d)
    ang = positions.astype(jnp.float32)[..., None] * inv_freq
    cos = jnp.cos(ang)[:, :, None, :]
    sin = jnp.sin(ang)[:, :, None, :]
    x32 = x.astype(jnp.float32)
    x1, x2 = x32[..., : d // 2], x32[..., d // 2:]
    out = jnp.concatenate([x1 * cos - x2 * sin, x2 * cos + x1 * sin], axis=-1)
    return out.astype(x.dtype)

def moba_attention(q, k, v):
    B, S, H, Dh = q.shape
    nb = -(-S // MOBA_BLOCK)
    n_sel = min(MOBA_TOPK, nb)
    pad = nb * MOBA_BLOCK - S
    kp = jnp.pad(k, ((0, 0), (0, pad), (0, 0), (0, 0)))
    vp = jnp.pad(v, ((0, 0), (0, pad), (0, 0), (0, 0)))
    kb = kp.reshape(B, nb, MOBA_BLOCK, H, Dh).transpose(0, 3, 1, 2, 4)
    vb = vp.reshape(B, nb, MOBA_BLOCK, H, Dh).transpose(0, 3, 1, 2, 4)
    k_mean = jnp.mean(kb.astype(jnp.float32), axis=3)
    scale = Dh ** -0.5
    bidx = jnp.arange(B)[:, None, None, None]
    hidx = jnp.arange(H)[None, None, :, None]

    def chunk(c):
        start = c * MOBA_Q_CHUNK
        qc = lax.dynamic_slice_in_dim(q, start, MOBA_Q_CHUNK, axis=1)
        blk = start // MOBA_BLOCK
        qpos = start + jnp.arange(MOBA_Q_CHUNK)
        gate = jnp.einsum('bqhd,bhnd->bqhn', qc.astype(jnp.float32), k_mean)
        past = jnp.arange(nb) < blk
        gate = jnp.where(past[None, None, None, :], gate, -jnp.inf)
        _, sel = lax.top_k(gate, n_sel)
        sel_valid = jnp.arange(n_sel) < blk
        k_sel = kb[bidx, hidx, sel]
        v_sel = vb[bidx, hidx, sel]
        s_sel = jnp.einsum('bqhd,bqhkjd->bqhkj', qc, k_sel).astype(jnp.float32) * scale
        s_sel = jnp.where(sel_valid[None, None, None, :, None], s_sel, -jnp.inf)
        s_sel = s_sel.reshape(B, MOBA_Q_CHUNK, H, n_sel * MOBA_BLOCK)
        k_own = lax.dynamic_slice_in_dim(kp, blk * MOBA_BLOCK, MOBA_BLOCK, axis=1)
        v_own = lax.dynamic_slice_in_dim(vp, blk * MOBA_BLOCK, MOBA_BLOCK, axis=1)
        s_own = jnp.einsum('bqhd,bjhd->bqhj', qc, k_own).astype(jnp.float32) * scale
        kpos = blk * MOBA_BLOCK + jnp.arange(MOBA_BLOCK)
        causal = kpos[None, :] <= qpos[:, None]
        s_own = jnp.where(causal[None, :, None, :], s_own, -jnp.inf)
        p = jax.nn.softmax(jnp.concatenate([s_sel, s_own], axis=-1), axis=-1).astype(v.dtype)
        p_sel = p[..., : n_sel * MOBA_BLOCK].reshape(B, MOBA_Q_CHUNK, H, n_sel, MOBA_BLOCK)
        p_own = p[..., n_sel * MOBA_BLOCK:]
        return (jnp.einsum('bqhkj,bqhkjd->bqhd', p_sel, v_sel)
                + jnp.einsum('bqhj,bjhd->bqhd', p_own, v_own))

    outs = lax.map(chunk, jnp.arange(S // MOBA_Q_CHUNK))
    return outs.transpose(1, 0, 2, 3, 4).reshape(B, S, H, Dh)

def mla_attention(q_nope, q_rope, k_nope, k_rope, v):
    B, S, H, _ = q_nope.shape
    scale = (MLA_NOPE_DIM + MLA_ROPE_DIM) ** -0.5
    kpos = jnp.arange(S)

    def block(c):
        start = c * MLA_Q_BLOCK
        qn = lax.dynamic_slice_in_dim(q_nope, start, MLA_Q_BLOCK, axis=1)
        qr = lax.dynamic_slice_in_dim(q_rope, start, MLA_Q_BLOCK, axis=1)
        s = (jnp.einsum('bqhd,bkhd->bhqk', qn, k_nope)
             + jnp.einsum('bqhd,bkd->bhqk', qr, k_rope)).astype(jnp.float32) * scale
        qpos = start + jnp.arange(MLA_Q_BLOCK)
        s = jnp.where((kpos[None, :] <= qpos[:, None])[None, None], s, -jnp.inf)
        p = jax.nn.softmax(s, axis=-1).astype(v.dtype)
        return jnp.einsum('bhqk,bkhd->bqhd', p, v)

    outs = lax.map(block, jnp.arange(S // MLA_Q_BLOCK))
    return outs.transpose(1, 0, 2, 3, 4).reshape(B, S, H * MLA_V_DIM)

def first_inputs(seed: int = 0) -> dict:
    key = jax.random.key(seed)
    ks = jax.random.split(key, 17)

    def dense(k, shape, fan_in):
        return jax.random.normal(k, shape, jnp.float32) * (fan_in ** -0.5)

    def gain(k, shape):
        return 1.0 + 0.02 * jax.random.normal(k, shape, jnp.float32)

    L = DEPTH
    return {
        "x": jax.random.normal(ks[0], (BATCH, SEQ, D_MODEL), jnp.float32),
        "positions": jnp.broadcast_to(jnp.arange(SEQ, dtype=jnp.int32), (BATCH, SEQ)),
        "attn_norm": gain(ks[1], (L, D_MODEL)),
        "w_in": dense(ks[2], (L, D_MODEL, IN_COLS), D_MODEL),
        "q_norm": gain(ks[3], (L, MLA_Q_RANK)),
        "w_uq": dense(ks[4], (L, MLA_Q_RANK, MLA_HEADS * (MLA_NOPE_DIM + MLA_ROPE_DIM)), MLA_Q_RANK),
        "kv_norm": gain(ks[5], (L, MLA_KV_RANK)),
        "w_ukv": dense(ks[6], (L, MLA_KV_RANK, MLA_HEADS * (MLA_NOPE_DIM + MLA_V_DIM)), MLA_KV_RANK),
        "w_branch_a": dense(ks[7], (L, MOBA_WIDTH, D_MODEL), MOBA_WIDTH),
        "w_branch_b": dense(ks[8], (L, MLA_WIDTH, D_MODEL), MLA_WIDTH),
        "w_out": dense(ks[9], (L, D_MODEL, D_MODEL), D_MODEL),
        "ffn_norm": gain(ks[10], (L, D_MODEL)),
        "w_gate": dense(ks[11], (L, D_MODEL, D_FF), D_MODEL),
        "w_up": dense(ks[12], (L, D_MODEL, D_FF), D_MODEL),
        "w_down": dense(ks[13], (L, D_FF, D_MODEL), D_FF),
        "final_norm": gain(ks[14], (D_MODEL,)),
    }

def first_block(x, positions, attn_norm, w_in, q_norm, w_uq, kv_norm, w_ukv, w_branch_a, w_branch_b,
              w_out, ffn_norm, w_gate, w_up, w_down, final_norm):
    B, S, _ = x.shape
    split_at = np.cumsum(np.array(IN_SIZES))[:-1].tolist()
    h = x
    for l in range(DEPTH):
        xn = rmsnorm(h, attn_norm[l])
        proj = xn @ w_in[l]
        q_a, k_a, v_a, c_q, c_kv, k_r, gates = jnp.split(proj, split_at, axis=-1)

        q_a = q_a.reshape(B, S, MOBA_HEADS, MOBA_HEAD_DIM)
        k_a = k_a.reshape(B, S, MOBA_HEADS, MOBA_HEAD_DIM)
        v_a = v_a.reshape(B, S, MOBA_HEADS, MOBA_HEAD_DIM)
        q_a = jnp.concatenate([rope(q_a[..., :PARTIAL_ROPE_DIM], positions), q_a[..., PARTIAL_ROPE_DIM:]], axis=-1)
        k_a = jnp.concatenate([rope(k_a[..., :PARTIAL_ROPE_DIM], positions), k_a[..., PARTIAL_ROPE_DIM:]], axis=-1)
        y_a = moba_attention(q_a, k_a, v_a).reshape(B, S, MOBA_WIDTH)

        qh = (rmsnorm(c_q, q_norm[l]) @ w_uq[l]).reshape(B, S, MLA_HEADS, MLA_NOPE_DIM + MLA_ROPE_DIM)
        q_nope, q_rope = qh[..., :MLA_NOPE_DIM], rope(qh[..., MLA_NOPE_DIM:], positions)
        kv = (rmsnorm(c_kv, kv_norm[l]) @ w_ukv[l]).reshape(B, S, MLA_HEADS, MLA_NOPE_DIM + MLA_V_DIM)
        k_nope, v_b = kv[..., :MLA_NOPE_DIM], kv[..., MLA_NOPE_DIM:]
        k_rope = rope(k_r[:, :, None, :], positions)[:, :, 0, :]
        y_b = mla_attention(q_nope, q_rope, k_nope, k_rope, v_b)

        g = jax.nn.sigmoid(gates.astype(jnp.float32)).astype(x.dtype)
        g_a, g_b = g[..., :D_MODEL], g[..., D_MODEL:]
        mixed = g_a * (y_a @ w_branch_a[l]) + g_b * (y_b @ w_branch_b[l])
        h = h + mixed @ w_out[l]

        hn = rmsnorm(h, ffn_norm[l])
        h = h + (jax.nn.silu(hn @ w_gate[l]) * (hn @ w_up[l])) @ w_down[l]
    return rmsnorm(h, final_norm)


N_MIXERS = 4
HEAD_DIM = 64
N_HEADS = D_MODEL // HEAD_DIM
N_KV_HEADS = N_HEADS // 4
GQA_GROUP = N_HEADS // N_KV_HEADS
WINDOW = 128
Q_BLOCK = 128
DIFF_HEADS = D_MODEL // (2 * HEAD_DIM)
DIFF_V_DIM = 2 * HEAD_DIM
HGRN_HEAD_DIM = 128
HGRN_HEADS = D_MODEL // HGRN_HEAD_DIM
HGRN_CHUNK = 64
IDX_HEADS = 16
IDX_DIM = 64
TOPK_MAX = 256
D_FF_2 = 5632
CONV_WIDTH = 3
NUM_BUCKETS = 32
MAX_DISTANCE = 128
RMS_EPS = 1e-6
N_SWA = len(range(0, DEPTH, N_MIXERS))
N_DIFF = len(range(1, DEPTH, N_MIXERS))
N_HGRN = len(range(2, DEPTH, N_MIXERS))
N_DSA = len(range(3, DEPTH, N_MIXERS))
SWA_SPLITS = (N_HEADS * HEAD_DIM, N_KV_HEADS * HEAD_DIM, N_KV_HEADS * HEAD_DIM)
SWA_IN = sum(SWA_SPLITS)
DIFF_SPLITS = (DIFF_HEADS * 2 * HEAD_DIM, DIFF_HEADS * 2 * HEAD_DIM, DIFF_HEADS * DIFF_V_DIM)
DIFF_IN = sum(DIFF_SPLITS)
HGRN_IN = 4 * HGRN_HEADS * HGRN_HEAD_DIM
DSA_SPLITS = (N_HEADS * HEAD_DIM, N_KV_HEADS * HEAD_DIM, N_KV_HEADS * HEAD_DIM,
              IDX_HEADS * IDX_DIM, IDX_DIM, IDX_HEADS)
DSA_IN = sum(DSA_SPLITS)


def split_cols(z, sizes):
    return jnp.split(z, [int(c) for c in np.cumsum(sizes)[:-1]], axis=-1)

def rms_norm(x, g):
    xf = x.astype(jnp.float32)
    y = xf * lax.rsqrt(jnp.mean(xf * xf, axis=-1, keepdims=True) + RMS_EPS)
    return (y * g.astype(jnp.float32)).astype(x.dtype)

def rel_position_bias(dist, table):
    n = jnp.maximum(dist, 0)
    max_exact = NUM_BUCKETS // 2
    log_ratio = jnp.log(jnp.maximum(n, 1).astype(jnp.float32) / max_exact) / math.log(MAX_DISTANCE / max_exact)
    large = jnp.minimum(max_exact + (log_ratio * (NUM_BUCKETS - max_exact)).astype(jnp.int32), NUM_BUCKETS - 1)
    bucket = jnp.where(n < max_exact, n, large)
    return table.astype(jnp.float32)[bucket]

def swa_sink_attention(h, w_in, w_out, sinks, bias_table):
    B, S, _ = h.shape
    nb = S // Q_BLOCK
    q, k, v = split_cols(h @ w_in, SWA_SPLITS)
    q = q.reshape(B, nb, Q_BLOCK, N_KV_HEADS, GQA_GROUP, HEAD_DIM)
    pad = ((0, 0), (Q_BLOCK, 0), (0, 0))
    kp = jnp.pad(k, pad).reshape(B, nb + 1, Q_BLOCK, N_KV_HEADS, HEAD_DIM)
    vp = jnp.pad(v, pad).reshape(B, nb + 1, Q_BLOCK, N_KV_HEADS, HEAD_DIM)
    kb = jnp.concatenate([kp[:, :-1], kp[:, 1:]], axis=2)
    vb = jnp.concatenate([vp[:, :-1], vp[:, 1:]], axis=2)
    qi = jnp.arange(Q_BLOCK)
    kj = jnp.arange(2 * Q_BLOCK) - Q_BLOCK
    dist = qi[:, None] - kj[None, :]
    in_band = (dist >= 0) & (dist < WINDOW)
    key_exists = (jnp.arange(nb)[:, None] > 0) | (kj[None, :] >= 0)
    mask = in_band[None] & key_exists[:, None, :]
    bias = rel_position_bias(dist, bias_table).transpose(2, 0, 1).reshape(
        N_KV_HEADS, GQA_GROUP, Q_BLOCK, 2 * Q_BLOCK)
    s = jnp.einsum('bnqhgd,bnshd->bnhgqs', q, kb).astype(jnp.float32) * HEAD_DIM ** -0.5 + bias
    s = jnp.where(mask[None, :, None, None], s, -jnp.inf)
    sink = jnp.broadcast_to(sinks.astype(jnp.float32).reshape(N_KV_HEADS, GQA_GROUP, 1, 1),
                            s.shape[:-1] + (1,))
    p = jax.nn.softmax(jnp.concatenate([s, sink], axis=-1), axis=-1)[..., :-1]
    o = jnp.einsum('bnhgqs,bnshd->bnqhgd', p.astype(vb.dtype), vb)
    return o.reshape(B, S, N_HEADS * HEAD_DIM) @ w_out

def diff_attention(h, w_in, w_out, lambdas, subln_g, bias_table, layer_idx):
    B, S, _ = h.shape
    nb = S // Q_BLOCK
    q, k, v = split_cols(h @ w_in, DIFF_SPLITS)
    q = q.reshape(B, nb, Q_BLOCK, DIFF_HEADS, 2, HEAD_DIM).transpose(1, 0, 2, 3, 4, 5)
    k = k.reshape(B, S, DIFF_HEADS, 2, HEAD_DIM)
    v = v.reshape(B, S, DIFF_HEADS, DIFF_V_DIM)
    lam_init = 0.8 - 0.6 * math.exp(-0.3 * layer_idx)
    lf = lambdas.astype(jnp.float32)
    lam = jnp.exp(jnp.sum(lf[0] * lf[1])) - jnp.exp(jnp.sum(lf[2] * lf[3])) + lam_init
    kpos = jnp.arange(S)

    def block(args):
        qb, start = args
        dist = (start + jnp.arange(Q_BLOCK))[:, None] - kpos[None, :]
        bias = rel_position_bias(dist, bias_table).reshape(Q_BLOCK, S, DIFF_HEADS, 2).transpose(2, 3, 0, 1)
        s = jnp.einsum('bqhmd,bshmd->bhmqs', qb, k).astype(jnp.float32) * HEAD_DIM ** -0.5 + bias
        p = jax.nn.softmax(jnp.where(dist >= 0, s, -jnp.inf), axis=-1)
        a = p[:, :, 0] - lam * p[:, :, 1]
        return jnp.einsum('bhqs,bshe->bqhe', a.astype(v.dtype), v)

    o = lax.map(block, (q, jnp.arange(nb) * Q_BLOCK))
    o = o.transpose(1, 0, 2, 3, 4).reshape(B, S, DIFF_HEADS, DIFF_V_DIM)
    o = rms_norm(o, subln_g) * (1.0 - lam_init)
    return o.reshape(B, S, DIFF_HEADS * DIFF_V_DIM) @ w_out

def hgrn2_recurrence(h, w_in, w_out, lb, norm_g):
    B, S, _ = h.shape
    nc = S // HGRN_CHUNK
    f32 = jnp.float32
    q, fz, i, g = jnp.split(h @ w_in, 4, axis=-1)

    def chunks(t):
        return t.astype(f32).reshape(B, nc, HGRN_CHUNK, HGRN_HEADS, HGRN_HEAD_DIM).transpose(1, 0, 3, 2, 4)

    lbf = lb.astype(f32)
    log_f = jnp.logaddexp(jnp.log(lbf), jnp.log1p(-lbf) + jax.nn.log_sigmoid(fz.astype(f32)))
    key = -jnp.expm1(log_f)
    qs, ks, vs, gs = chunks(jax.nn.silu(q.astype(f32))), chunks(key), chunks(i), chunks(log_f)
    causal = jnp.tril(jnp.ones((HGRN_CHUNK, HGRN_CHUNK), dtype=bool))

    def step(state, inp):
        qc, kc, vc, gc = inp
        b = jnp.cumsum(gc, axis=2)
        o_inter = jnp.einsum('bhtk,bhkv->bhtv', qc * jnp.exp(b), state)
        rel = jnp.where(causal[:, :, None], b[:, :, :, None, :] - b[:, :, None, :, :], -jnp.inf)
        att = jnp.einsum('bhtsk,bhsk->bhts', qc[:, :, :, None, :] * jnp.exp(rel), kc)
        o_intra = jnp.einsum('bhts,bhsv->bhtv', att, vc)
        b_end = b[:, :, -1:, :]
        state = state * jnp.exp(b_end[:, :, 0, :, None]) + jnp.einsum(
            'bhsk,bhsv->bhkv', kc * jnp.exp(b_end - b), vc)
        return state, o_inter + o_intra

    state0 = jnp.zeros((B, HGRN_HEADS, HGRN_HEAD_DIM, HGRN_HEAD_DIM), f32)
    _, o = lax.scan(step, state0, (qs, ks, vs, gs))
    o = o.transpose(1, 0, 3, 2, 4).reshape(B, S, HGRN_HEADS, HGRN_HEAD_DIM)
    gate = jax.nn.silu(g.astype(f32)).reshape(B, S, HGRN_HEADS, HGRN_HEAD_DIM)
    o = (rms_norm(o, norm_g) * gate).astype(h.dtype)
    return o.reshape(B, S, HGRN_HEADS * HGRN_HEAD_DIM) @ w_out

def dsa_sparse_attention(h, w_in, w_out, bias_table):
    B, S, _ = h.shape
    nb = S // Q_BLOCK
    n_sel = min(TOPK_MAX, S // 4)
    f32 = jnp.float32
    q, k, v, qi, ki, wi = split_cols(h @ w_in, DSA_SPLITS)
    q = q.reshape(B, nb, Q_BLOCK, N_KV_HEADS, GQA_GROUP, HEAD_DIM).transpose(1, 0, 2, 3, 4, 5)
    qi = qi.reshape(B, nb, Q_BLOCK, IDX_HEADS, IDX_DIM).transpose(1, 0, 2, 3, 4)
    wi = wi.reshape(B, nb, Q_BLOCK, IDX_HEADS).transpose(1, 0, 2, 3)
    k = k.reshape(B, S, N_KV_HEADS, HEAD_DIM)
    v = v.reshape(B, S, N_KV_HEADS, HEAD_DIM)
    kpos = jnp.arange(S)
    gather = jax.vmap(lambda t, idx: t[idx])

    def block(args):
        qb, qib, wib, start = args
        qpos = start + jnp.arange(Q_BLOCK)
        logits = jnp.einsum('bqhd,bsd->bqhs', qib, ki).astype(f32) * IDX_DIM ** -0.5
        score = jnp.einsum('bqh,bqhs->bqs', wib.astype(f32) * IDX_HEADS ** -0.5, jax.nn.relu(logits))
        score = jnp.where(qpos[:, None] >= kpos[None, :], score, -jnp.inf)
        _, idx = lax.top_k(score, n_sel)
        valid = idx <= qpos[None, :, None]
        kg, vg = gather(k, idx), gather(v, idx)
        s = jnp.einsum('bqhgd,bqkhd->bhgqk', qb, kg).astype(f32) * HEAD_DIM ** -0.5
        bias = rel_position_bias(qpos[None, :, None] - idx, bias_table).transpose(0, 3, 1, 2).reshape(
            B, N_KV_HEADS, GQA_GROUP, Q_BLOCK, n_sel)
        s = jnp.where(valid[:, None, None], s + bias, -jnp.inf)
        p = jax.nn.softmax(s, axis=-1)
        return jnp.einsum('bhgqk,bqkhd->bqhgd', p.astype(vg.dtype), vg)

    o = lax.map(block, (q, qi, wi, jnp.arange(nb) * Q_BLOCK))
    return o.transpose(1, 0, 2, 3, 4, 5).reshape(B, S, N_HEADS * HEAD_DIM) @ w_out

def conv_ffn(h, w_up, conv_w, w_down):
    S = h.shape[1]
    u = h @ w_up
    up = jnp.pad(u, ((0, 0), (CONV_WIDTH - 1, 0), (0, 0)))
    c = conv_w[0] * up[:, 0:S]
    for j in range(1, CONV_WIDTH):
        c = c + conv_w[j] * up[:, j:j + S]
    gate, val = jnp.split(c, 2, axis=-1)
    return (jax.nn.silu(gate) * val) @ w_down

def second_inputs(seed: int = 0) -> dict:
    key = jax.random.key(seed)
    ks = jax.random.split(key, 20)
    f32 = jnp.float32

    def dense(k, shape, fan_in):
        return jax.random.normal(k, shape, f32) * fan_in ** -0.5

    return {
        'x': jax.random.normal(ks[0], (BATCH, SEQ, D_MODEL), f32),
        'rel_bias_table': 0.3 * jax.random.normal(ks[1], (NUM_BUCKETS, N_HEADS), f32),
        'hgrn_lb_logits': 0.5 * jax.random.normal(ks[2], (DEPTH, HGRN_HEADS * HGRN_HEAD_DIM), f32),
        'norm_g': 1.0 + 0.02 * jax.random.normal(ks[3], (DEPTH, 4, D_MODEL), f32),
        'ffn_w_up': dense(ks[4], (DEPTH, D_MODEL, 2 * D_FF_2), D_MODEL),
        'ffn_conv': dense(ks[5], (DEPTH, CONV_WIDTH, 2 * D_FF_2), CONV_WIDTH),
        'ffn_w_down': dense(ks[6], (DEPTH, D_FF_2, D_MODEL), D_FF_2),
        'swa_w_in': dense(ks[7], (N_SWA, D_MODEL, SWA_IN), D_MODEL),
        'swa_w_out': dense(ks[8], (N_SWA, N_HEADS * HEAD_DIM, D_MODEL), N_HEADS * HEAD_DIM),
        'swa_sinks': 0.5 * jax.random.normal(ks[9], (N_SWA, N_HEADS), f32),
        'diff_w_in': dense(ks[10], (N_DIFF, D_MODEL, DIFF_IN), D_MODEL),
        'diff_w_out': dense(ks[11], (N_DIFF, DIFF_HEADS * DIFF_V_DIM, D_MODEL), DIFF_HEADS * DIFF_V_DIM),
        'diff_lambda': 0.1 * jax.random.normal(ks[12], (N_DIFF, 4, HEAD_DIM), f32),
        'diff_subln_g': 1.0 + 0.02 * jax.random.normal(ks[13], (N_DIFF, DIFF_V_DIM), f32),
        'hgrn_w_in': dense(ks[14], (N_HGRN, D_MODEL, HGRN_IN), D_MODEL),
        'hgrn_w_out': dense(ks[15], (N_HGRN, HGRN_HEADS * HGRN_HEAD_DIM, D_MODEL), HGRN_HEADS * HGRN_HEAD_DIM),
        'hgrn_norm_g': 1.0 + 0.02 * jax.random.normal(ks[16], (N_HGRN, HGRN_HEAD_DIM), f32),
        'dsa_w_in': dense(ks[17], (N_DSA, D_MODEL, DSA_IN), D_MODEL),
        'dsa_w_out': dense(ks[18], (N_DSA, N_HEADS * HEAD_DIM, D_MODEL), N_HEADS * HEAD_DIM),
    }

def second_block(x, rel_bias_table, hgrn_lb_logits, norm_g, ffn_w_up, ffn_conv, ffn_w_down,
              swa_w_in, swa_w_out, swa_sinks, diff_w_in, diff_w_out, diff_lambda, diff_subln_g,
              hgrn_w_in, hgrn_w_out, hgrn_norm_g, dsa_w_in, dsa_w_out):
    lb_soft = jax.nn.softmax(hgrn_lb_logits.astype(jnp.float32), axis=0)
    lb_all = jnp.cumsum(lb_soft, axis=0) - lb_soft[0]
    for i in range(DEPTH):
        kind, j = i % N_MIXERS, i // N_MIXERS
        h = rms_norm(x, norm_g[i, 0])
        if kind == 0:
            m = swa_sink_attention(h, swa_w_in[j], swa_w_out[j], swa_sinks[j], rel_bias_table)
        elif kind == 1:
            m = diff_attention(h, diff_w_in[j], diff_w_out[j], diff_lambda[j], diff_subln_g[j],
                               rel_bias_table, i)
        elif kind == 2:
            m = hgrn2_recurrence(h, hgrn_w_in[j], hgrn_w_out[j], lb_all[i], hgrn_norm_g[j])
        else:
            m = dsa_sparse_attention(h, dsa_w_in[j], dsa_w_out[j], rel_bias_table)
        x = x + rms_norm(m, norm_g[i, 1])
        h = rms_norm(x, norm_g[i, 2])
        x = x + rms_norm(conv_ffn(h, ffn_w_up[i], ffn_conv[i], ffn_w_down[i]), norm_g[i, 3])
    return x


def setup_inputs(seed=0):
    out = dict(first_inputs(seed))
    for name, value in second_inputs(seed + 1).items():
        if name != "x":
            out[name + "_2"] = value
    return out


def reference(
    x, positions, attn_norm, w_in, q_norm, w_uq, kv_norm, w_ukv, w_branch_a, w_branch_b, w_out,
    ffn_norm, w_gate, w_up, w_down, final_norm, rel_bias_table_2, hgrn_lb_logits_2, norm_g_2,
    ffn_w_up_2, ffn_conv_2, ffn_w_down_2, swa_w_in_2, swa_w_out_2, swa_sinks_2, diff_w_in_2,
    diff_w_out_2, diff_lambda_2, diff_subln_g_2, hgrn_w_in_2, hgrn_w_out_2, hgrn_norm_g_2,
    dsa_w_in_2, dsa_w_out_2,
):
    x = first_block(
        x, positions, attn_norm, w_in, q_norm, w_uq, kv_norm, w_ukv, w_branch_a, w_branch_b,
        w_out, ffn_norm, w_gate, w_up, w_down, final_norm,
    )
    return second_block(
        x, rel_bias_table_2, hgrn_lb_logits_2, norm_g_2, ffn_w_up_2, ffn_conv_2, ffn_w_down_2,
        swa_w_in_2, swa_w_out_2, swa_sinks_2, diff_w_in_2, diff_w_out_2, diff_lambda_2,
        diff_subln_g_2, hgrn_w_in_2, hgrn_w_out_2, hgrn_norm_g_2, dsa_w_in_2, dsa_w_out_2,
    )


_drawn_inputs = setup_inputs


def setup_inputs(seed=0):
    import zlib

    import numpy as np

    out = dict(_drawn_inputs(seed))
    spreads = {}
    factors = {'attn_norm': 4.994, 'q_norm': 8.0, 'kv_norm': 7.242, 'swa_sinks_2': 3.174, 'ffn_norm': 8.0}
    for name, (base, spread) in spreads.items():
        noise = np.random.default_rng([zlib.crc32(name.encode()), seed]).standard_normal(out[name].shape)
        drawn = base * np.exp(spread * noise) if base else spread * noise
        out[name] = __import__('jax').numpy.asarray(drawn.astype(out[name].dtype))
    for name, factor in factors.items():
        out[name] = (out[name] * factor).astype(out[name].dtype)
    return out
```

```python
import math
from contextlib import ExitStack

import numpy as np

import concourse.bass as bass
from concourse import mybir

F32 = mybir.dt.float32
F32R = mybir.dt.float32r
BF16 = mybir.dt.bfloat16
I32 = mybir.dt.int32
ALU = mybir.AluOpType
ACT = mybir.ActivationFunctionType
AX = mybir.AxisListType.X

P = 128
D = 2048
S = 256
KT = D // P
IN = 8000
FF = 5632
NF = FF // 512
FT = FF // P
EPS = 1e-6
NEG = -1.0e30
RAW = 4
PAIR = 3
MAGIC = 12582912.0


class Mark:
    __slots__ = ("used", "sem", "value")

    def __init__(self, sem=None, value=None):
        self.used, self.sem, self.value = False, sem, value


class Queue:

    def __init__(self, sem):
        self.sem, self.items = sem, []

    def do(self, fn, *after):
        m = Mark()
        self.items.append((fn, flat(after), m, 1))
        return m

    def dma(self, out, src, lane, *after, eng, **how):
        lane[1] += 16
        m = Mark(lane[0], lane[1])
        self.items.append((lambda: eng.dma_start(out, src, **how), flat(after), m, 16))
        return m

    def number(self):
        n = 0
        for _, _, m, inc in self.items:
            if inc == 1 and m.used:
                n += 1
                m.sem, m.value = self.sem, n

    def emit(self, eng):
        seen = {}
        for fn, after, m, inc in self.items:
            need = {}
            for a in after:
                if a.value > need.get(a.sem.name, (0, None))[0]:
                    need[a.sem.name] = (a.value, a.sem)
            for name, (value, sem) in need.items():
                if seen.get(name, 0) < value:
                    seen[name] = value
                    eng.wait_ge(sem, value)
            ins = fn()
            if inc == 16 or m.used:
                ins.then_inc(m.sem, inc)


def flat(xs):
    out = []
    for x in xs:
        if x is None:
            continue
        if isinstance(x, Mark):
            x.used = True
            out.append(x)
        else:
            out += flat(x)
    return out


class Buf:

    def __init__(self, ap):
        self.ap, self.free = ap, []


class Bufs:
    def __init__(self, aps):
        self.idle = [Buf(a) for a in aps]

    def take(self):
        return self.idle.pop(0) if self.idle else None

    def give(self, b, *marks):
        b.free = list(marks)
        self.idle.append(b)


def steps_of(cols, kt, a=2):
    return [(k, min(a, kt - k), n) for n in cols for k in range(0, kt, a)]


def build(nc, A):
    ctx = ExitStack()
    with ctx:
        def sb(name, shape, dt=F32):
            return ctx.enter_context(nc.sbuf_tensor(name, shape, dt))

        def region(name, floats):
            t = sb(name, [P, floats])
            return t, nc.sbuf_base - 4 * floats

        def at(name, reg, off, shape, dt=F32):
            return nc.alloc_sbuf_tensor_at(name, [P] + shape, dt, offset=reg + 4 * off)

        def sem(name):
            return ctx.enter_context(nc.semaphore(name))

        def lane(name):
            return [sem(name), 0]

        raw = sb("raw", [P, RAW, 1024])
        whi = sb("whi", [P, PAIR, 1024], F32R)
        wlo = sb("wlo", [P, PAIR, 1024], F32R)
        X = sb("X", [P, 2, D])
        _, rT = region("regT", 8192)
        _, rH = region("regH", 22528)
        _, rN = region("regN", 2048)
        _, rW = region("regW", 3072)
        Th = at("Th", rT, 0, [KT, S], F32R)
        Tl = at("Tl", rT, 4096, [KT, S], F32R)
        G = at("G", rH, 0, [4, 2, 2, 512])
        MT = at("MT", rH, 0, [4, 2, 4, S], F32R)
        YF = at("YF", rH, 8192, [16, S])
        CTh = at("CTh", rH, 12288, [6, S], F32R)
        CTl = at("CTl", rH, 13824, [6, S], F32R)
        QT = at("QT", rH, 15360, [8, S])
        KTt = at("KTt", rH, 17408, [8, S])
        V = at("V", rH, 19456, [2, 1024])
        QR = at("QR", rH, 21504, [4, S])
        KR = at("KR", rW, 2304, [2, S])
        S1 = at("S1", rW, 0, [4, 384])
        PT1 = at("PT1", rW, 1536, [2, 384])
        Hh = at("Hh", rH, 0, [FT, S], F32R)
        Hl = at("Hl", rH, 11264, [FT, S], F32R)
        SG = at("SG", rW, 0, [2, 512])
        HID = at("HID", rW, 1024, [2, 2, 512])
        U = at("U", rW, 0, [4, 258])
        SG2 = at("SG2", rW, 1032, [4, S])
        C = at("C", rW, 2056, [3, S])
        KK = at("KK", rH, 0, [8, 2, S])
        MG = at("MG", rH, 0, [2, D])
        VV = at("VV", rH, 4096, [2, 8, 2, 64])
        QP = at("QP", rH, 6144, [2, 4, S])
        YH = at("YH", rH, 8192, [16, S], F32R)
        YL = at("YL", rH, 12288, [16, S], F32R)
        BT = at("BT", rH, 16384, [2, 8, S])
        S2a = at("S2a", rH, 20480, [2, 768])
        S2b = at("S2b", rW, 0, [2, 768])
        PT2 = at("PT2", rW, 1536, [2, 768])
        MG2 = at("MG2", rT, 0, [2, D])
        NAT = at("NAT", rN, 0, [2, 1024])
        GB = at("GB", rN, 0, [D])
        STG = at("STG", rN, 0, [4, P])
        ident = sb("ident", [P, P])
        mask = sb("mask", [P, 384])
        freq = sb("freq", [P, 48])
        CS = sb("CS", [P, 2, 96])
        SN = sb("SN", [P, 2, 96])
        GT = sb("GT", [P, 118])
        GFN = sb("GFN", [P, 16])
        CW = sb("CW", [P, 3, 88])
        SK = sb("SK", [P, 32])
        ST = sb("ST", [P, 144])
        AS = sb("AS", [P, 6, 16])
        JK = sb("JK", [P, 512], BF16)
        RA = sb("RA", [P, 2, P])
        RB = sb("RB", [P, 2, P])
        RP = sb("RP", [P, 2, P])
        PI = sb("PI", [P, 2], I32)

        banks = [ctx.enter_context(nc.psum_tensor(f"bank{i}", [P, 512], F32)) for i in range(8)]
        lines = nc.dram_tensor("bias_lines", [32, 384], F32)

        pe, act, dve, pool = (Queue(sem(f"s_{n}")) for n in ("pe", "act", "dve", "pool"))
        sp = Queue(None)
        l_raw = [lane(f"l_raw{i}") for i in range(RAW)]
        l_x = [lane(f"l_x{i}") for i in range(4)]
        l_out = lane("l_out")

        def load(out, src, name, *after, q=sp, eng=nc.sync, **how):
            return q.dma(out, src, lane(name), *after, eng=eng, **how)

        def a_copy(out, src, *after, scale=1.0):
            return act.do(lambda: nc.scalar.activation(out, src, ACT.Copy, scale=scale), *after)

        def a_fn(fn, out, src, *after, scale=1.0, bias=0.0, acc=None):
            if acc is None:
                return act.do(lambda: nc.scalar.activation(out, src, fn, bias=bias, scale=scale), *after)
            return act.do(lambda: nc.scalar.activation(out, src, fn, bias=bias, scale=scale, accum_out=acc), *after)

        def v_tt(out, a, b, op, *after):
            return dve.do(lambda: nc.vector.tensor_tensor(out, a, b, op), *after)

        def v_ts(out, a, s1, s2, op0, op1, *after):
            if s2 is None:
                return dve.do(lambda: nc.vector.tensor_scalar(out, a, s1, None, op0), *after)
            return dve.do(lambda: nc.vector.tensor_scalar(out, a, s1, s2, op0, op1), *after)

        def v_stt(out, a, s, b, op0, op1, *after):
            return dve.do(lambda: nc.vector.scalar_tensor_tensor(out=out, in0=a, scalar=s, in1=b, op0=op0, op1=op1), *after)

        def v_max(out, a, *after):
            return dve.do(lambda: nc.vector.reduce_max(out, a, AX), *after)

        def p_mm(list_, *after):
            def go():
                for out, lhsT, rhs, start, stop in list_:
                    last = nc.tensor.matmul(out, lhsT, rhs, start=start, stop=stop)
                return last
            return pe.do(go, *after)

        def p_tr(list_, *after):
            def go():
                for out, in_ in list_:
                    last = nc.tensor.transpose(out, in_, ident[:, :])
                return last
            return pe.do(go, *after, m_ident)

        pool_last = [None]

        def on_pool(fn, *after):
            pool_last[0] = pool.do(fn, after, pool_last[0])
            return pool_last[0]

        def r32(ap):
            return ap.bitcast(F32)

        main = Bufs([b[:, :] for b in banks[0:4]])
        side = Bufs([b[:, :] for b in banks[4:8]])

        tasks = []

        def later(g, n):
            for _ in range(n):
                yield
            yield from g

        def spawn(g, wait=1):
            tasks.append(later(g, wait) if wait else g)

        def pump():
            for g in list(tasks):
                if next(g, "end") == "end":
                    tasks.remove(g)

        def force(done):
            n = 0
            while not done():
                pump()
                n += 1
                assert n < 1000, "a task never ends"

        def takes(bufs):
            while True:
                b = bufs.take()
                if b is not None:
                    return b
                yield

        w = {n: A[n].rearrange("l (k p) n -> (l p) k n", p=P) for n in (
            "w_in", "w_uq", "w_ukv", "w_branch_a", "w_branch_b", "w_out", "w_gate", "w_up", "w_down",
            "swa_w_in_2", "swa_w_out_2", "ffn_w_up_2", "ffn_w_down_2")}
        jobs = []

        def product(name, groups, kt, order=None):
            steps = order or [(i, k, min(2, kt - k)) for i in range(len(groups)) for k in range(0, kt, 2)]
            for i, k, a in steps:
                c, n = groups[i]
                jobs.append((w[name][:, k:k + a, c:c + n], a, n))
            return steps

        jc = [product("w_in", [(3072, 512), (3584, 320)], KT)]
        jqkv = product("w_in", [(512 * i, 512) for i in range(6)], KT)
        gcols = [(3904 + D * ab + 512 * n, 512) for n in range(4) for ab in range(2)]
        jg1 = product("w_in", gcols[:4], KT)
        juq = product("w_uq", [(384 * i, 384) for i in range(4)], 4)
        jukv = product("w_ukv", [(512 * i, 512) for i in range(4)], 2)
        jg2 = product("w_in", gcols[4:], KT)
        n4 = [(512 * i, 512) for i in range(4)]
        jbr = []
        for i in range(4):
            jbr.append((product("w_branch_a", n4[i:i + 1], 8), product("w_branch_b", n4[i:i + 1], 8)))
        jout = product("w_out", n4, KT)
        jff = []
        for i in range(NF):
            c = [(512 * i, 512)]
            jff.append((product("w_gate", c, KT), product("w_up", c, KT)))
        jdown = product("w_down", n4, FT)
        icols = [(2048, 512), (2560, 512)] + n4
        jin2 = product("swa_w_in_2", icols, KT)
        split_at = 12
        oorder = [(i, k, 2) for i in (0, 1) for k in range(0, split_at, 2)]
        oorder += [(i, k, 2) for i in (0, 1) for k in range(split_at, KT, 2)]
        oorder += [(i, k, 2) for i in (2, 3) for k in range(0, KT, 2)]
        jout2 = product("swa_w_out_2", n4, KT, oorder)
        jff2 = []
        for i in range(NF):
            jff2.append((product("ffn_w_up_2", [(512 * i, 512)], KT),
                         product("ffn_w_up_2", [(FF + 512 * i, 512)], KT)))
        jdown2 = product("ffn_w_down_2", n4, FT)

        at_job = {"fetch": 0, "split": 0, "use": 0}
        split_hi, split_lo, used = [], [], []

        def fetch():
            i = at_job["fetch"]
            if i >= len(jobs):
                return
            src, a, n = jobs[i]
            before = [split_hi[i - RAW], split_lo[i - RAW]] if i >= RAW else None
            out = raw[:, i % RAW, 0:a * n].rearrange("p (a n) -> p a n", a=a)
            fetched.append(sp.dma(out, src, l_raw[i % RAW], before, eng=nc.sync))
            at_job["fetch"] += 1

        fetched = []

        def split():
            i = at_job["split"]
            if i >= len(jobs):
                return
            _, a, n = jobs[i]
            before = used[i - PAIR] if i >= PAIR else None
            src = raw[:, i % RAW, 0:a * n]
            hi, lo = whi[:, i % PAIR, 0:a * n], wlo[:, i % PAIR, 0:a * n]
            split_hi.append(act.do(lambda: nc.scalar.copy(hi, src), fetched[i], before))
            split_lo.append(v_tt(lo, src, r32(hi), ALU.subtract, split_hi[i], before))
            at_job["split"] += 1
            fetch()

        def chunk():
            i = at_job["use"]
            while at_job["split"] <= min(i + PAIR - 1, len(jobs) - 1):
                split()
            at_job["use"] += 1
            _, a, n = jobs[i]
            hi = whi[:, i % PAIR, 0:a * n].rearrange("p (a n) -> p a n", a=a)
            lo = wlo[:, i % PAIR, 0:a * n].rearrange("p (a n) -> p a n", a=a)
            return hi, lo, split_lo[i]

        def gemm(steps, kt, cols, left, evac):
            taken, seen_k = {}, {}
            for i, k0, a in steps:
                hi, lo, m_w = chunk()
                if i not in taken:
                    taken[i] = (main.take(), main.take())
                    seen_k[i] = 0
                bk = taken[i]
                for kk in range(a):
                    lh, ll, m_l = left(k0 + kk)
                    n = cols
                    mms = []
                    first, last = seen_k[i] == 0, seen_k[i] == kt - 1
                    for t in range(2):
                        o, ts = bk[t].ap[:, 0:n], slice(t * P, (t + 1) * P)
                        mms += [(o, lh[:, ts], hi[:, kk, :], first, False),
                                (o, lh[:, ts], lo[:, kk, :], False, False),
                                (o, ll[:, ts], hi[:, kk, :], False, last)]
                    m = p_mm(mms, m_w, m_l, [bk[0].free, bk[1].free] if first else None)
                    seen_k[i] += 1
                used.append(m)
                if seen_k[i] == kt:
                    evac(i, bk, m)
                pump()
            return m

        ready = {}

        def done(key):
            if key not in ready:
                force(lambda: key in ready)
            return ready[key]

        def from_T(k):
            m = done(("T", k))
            return Th[:, k, :], Tl[:, k, :], m

        def to_parts(name, src, m_src, dst, ks, gain, free=None, after=None):
            ks = list(ks)
            groups = [ks[i:i + 2] for i in range(0, len(ks), 2)]
            n = 0
            held = []
            for g in groups:
                b = yield from takes(side)
                mt = p_tr([(b.ap[:, kk * S + t * P:kk * S + (t + 1) * P], src(n + kk, t))
                           for kk in range(len(g)) for t in range(2)], b.free, m_src)
                held.append((b, g, mt))
                n += len(g)
                if len(side.idle) == 0:
                    break
            trans = [h[2] for h in held]
            if after is not None:
                assert len(held) == len(groups)
                after(trans)
            yield
            while held:
                b, g, mt = held.pop(0)
                ah = []
                for kk, k in enumerate(g):
                    h, _ = dst(k)
                    sc = 1.0 if gain is None else gain[:, k:k + 1]
                    ah.append(a_copy(h, b.ap[:, kk * S:(kk + 1) * S], mt, trans, free, scale=sc))
                ms = []
                for kk, k in enumerate(g):
                    h, lo = dst(k)
                    if gain is None:
                        ms.append(v_tt(lo, b.ap[:, kk * S:(kk + 1) * S], r32(h), ALU.subtract, ah))
                    else:
                        ms.append(v_stt(lo, b.ap[:, kk * S:(kk + 1) * S], gain[:, k:k + 1], r32(h),
                                        ALU.mult, ALU.subtract, ah))
                    ready[(name, k)] = [ah[kk], ms[-1]]
                side.give(b, ms)
                if n < len(ks):
                    g = groups[n // 2]
                    b = yield from takes(side)
                    mt = p_tr([(b.ap[:, kk * S + t * P:kk * S + (t + 1) * P], src(n + kk, t))
                               for kk in range(len(g)) for t in range(2)], b.free, m_src)
                    held.append((b, g, mt))
                    trans.append(mt)
                    n += len(g)
                    yield

        st_at = [0]

        def stat(n):
            st_at[0] += n
            return ST[:, st_at[0] - n:st_at[0]]

        junk = [None]

        def square(src, acc, *after):
            junk[0] = a_fn(ACT.Square, JK[:, 0:src.shape[-1]], src, after, junk[0], acc=acc)
            return junk[0]

        def rstd_of(ss, n, width, out, *after):
            mean = stat(2)
            m = dve.do(lambda: nc.vector.reduce_sum(mean, ss.rearrange("p (t n) -> p t n", n=n), AX), after)
            m = v_ts(mean, mean, 1.0 / width, EPS, ALU.mult, ALU.add, m)
            return on_pool(lambda: nc.gpsimd.tensor_tensor(out, mean, mhalf, ALU.pow), m, m_half)

        m_ident = load(ident[:, :], A["c_main"][:, 0:128], "l_ident")
        mhalf = stat(2)
        m_half = on_pool(lambda: nc.gpsimd.memset(mhalf, -0.5))
        m_z = on_pool(lambda: nc.gpsimd.memset(STG[:, :, :], 0.0))
        stage = lane("l_stage")
        r0 = 0
        m_stage = []
        for nm, rows in (("attn_norm", 16), ("ffn_norm", 16), ("final_norm", 16), ("norm_g_2", 64),
                         ("q_norm", 4), ("kv_norm", 2)):
            src = A[nm]
            src = {1: lambda s: s.rearrange("(k p) -> k p", p=P),
                   2: lambda s: s.rearrange("l (k p) -> (l k) p", p=P),
                   3: lambda s: s.rearrange("l g (k p) -> (l g k) p", p=P)}[len(src.shape)](src)
            m_stage.append(sp.dma(STG[r0:r0 + rows, 0, :], src, stage, m_z, eng=nc.sync))
            r0 += rows
        for j in range(3):
            m_stage.append(sp.dma(STG[0:88, 1 + j, :], A["ffn_conv_2"][0, j].rearrange("(k p) -> k p", p=P),
                                  stage, m_z, eng=nc.sync))
        m_staged = m_stage[-1]
        x_v = A["x"].rearrange("b (t p) d -> p (b t) d", p=P)
        m_x = [sp.dma(X[:, :, 512 * c:512 * (c + 1)], x_v[:, :, 512 * c:512 * (c + 1)], l_x[c], eng=nc.sync)
               for c in range(4)]
        for _ in range(RAW):
            fetch()
        m_mask = load(mask[:, :], A["c_main"][:, 128:512], "l_mask")
        m_freq = load(freq[:, :], A["c_main"][:, 512:560], "l_freq")
        m_pos = load(PI[:, :], A["positions"].rearrange("b (t p) -> p (b t)", p=P), "l_pos",
                     allow_slow_non_contiguous=True)
        tb = RA[0:32, 0, 0:32]
        oh = SG[0:32, 0, 0:384]
        ng = SG[0:32, 1, 0:384]
        m_tb = load(tb, A["rel_bias_table_2"], "l_tb")
        m_oh = load(oh, A["c_bias"][:, 0:384], "l_oh")
        m_ng = load(ng, A["c_bias"][:, 384:768], "l_ng")
        m_sk = load(SK[:, :], bass.AP(A["swa_sinks_2"].tensor, 0, [[0, P], [1, 32]]), "l_sk")

        b = side.take()
        mt = p_tr([(b.ap[:, j * P:(j + 1) * P], STG[:, j, :]) for j in range(4)], m_staged)
        m = a_copy(GT[:, :], b.ap[:, 0:118], mt)
        m_cw = a_copy(CW[:, :, :], b.ap[:, P:512].rearrange("p (j k) -> p j k", j=3)[:, :, 0:88], mt)
        side.give(b, m_cw)
        m_gt = m
        m_gfn = v_tt(GFN[:, :], GT[:, 32:48], GT[:, 48:64], ALU.mult, m_gt)
        m_nat0 = mt

        def T_dst(k):
            return Th[:, k, :], Tl[:, k, :]

        for c in range(4):
            spawn(to_parts("T", lambda i, t, c=c: X[:, t, (4 * c + i) * P:(4 * c + i + 1) * P], m_x[c],
                           T_dst, range(4 * c, 4 * c + 4), GT[:, 0:16], free=m_gt), 0)
        rs_x = stat(2)

        def first_norm():
            ss = stat(8)
            m_ss = []
            for c in range(4):
                for t in range(2):
                    yield
                    m_ss.append(square(X[:, t, 512 * c:512 * (c + 1)], ss[:, 4 * t + c:4 * t + c + 1], m_x[c]))
            ready["rs_x"] = rstd_of(ss, 4, D, rs_x, m_ss)
        spawn(first_norm(), 0)

        W96 = [RB[:, 0, 0:96], RB[:, 1, 0:96], RP[:, 0, 0:96], RP[:, 1, 0:96]]
        ang, nn, sn, cs = W96
        pf = stat(2)
        two_pi = 2 * math.pi

        def pieces(v, n):
            out = []
            for _ in range(n):
                e = math.floor(math.log2(abs(v)))
                q = 2.0 ** (e - 11)
                p = math.floor(v / q) * q
                out.append(p)
                v -= p
            return out

        m_trig = []

        def trig():
            m = dve.do(lambda: nc.vector.tensor_copy(pf, PI[:, :]), m_pos)
            for t in range(2):
                m2 = v_ts(ang[:, 48 * t:48 * t + 48], freq[:, :], pf[:, t:t + 1], None, ALU.mult, None, m, m_freq)
            m = m2
            for scale in (1024.0, 1.0):
                m = v_ts(nn, ang, 1.0 / (two_pi * scale), MAGIC, ALU.mult, ALU.add, m)
                m = v_ts(nn, nn, -MAGIC, None, ALU.add, None, m)
                yield
                for p in pieces(two_pi, 4):
                    m = v_stt(ang, nn, -p * scale, ang, ALU.mult, ALU.add, m)
            yield
            PIF = 3.1415925
            m_ang = v_ts(ang, ang, PIF, -PIF, ALU.min, ALU.max, m)
            m_sin = a_fn(ACT.Sin, sn, ang, m_ang)
            m = v_ts(nn, ang, -1.0, None, ALU.mult, None, m_ang)
            m = v_tt(nn, nn, ang, ALU.max, m)
            m = v_ts(nn, nn, -1.0, math.pi / 2, ALU.mult, ALU.add, m)
            m_cos = a_fn(ACT.Sin, cs, nn, m)
            c3, s3 = (z.rearrange("p (t f) -> p t f", t=2) for z in (cs, sn))
            for f0, d, o in ((0, 16, 0), (16, 32, 32)):
                for h, sign in ((0, -1.0), (1, 1.0)):
                    oo = slice(o + h * d, o + h * d + d)
                    m_trig.append(v_ts(CS[:, :, oo], c3[:, :, f0:f0 + d], 1.0, None, ALU.mult, None, m_cos))
                    m_trig.append(v_ts(SN[:, :, oo], s3[:, :, f0:f0 + d], sign, None, ALU.mult, None, m_sin))
            ready["trig"] = m_trig
        spawn(trig(), 3)

        def bias_lines():
            b = yield from takes(side)
            mm = p_mm([(b.ap[0:32, 0:384], tb, oh, True, True)], m_tb, m_oh, b.free)
            yield
            ml = v_tt(oh, b.ap[0:32, 0:384], ng, ALU.add, mm, m_ng)
            side.give(b, ml)
            ready["lines"] = load(lines[:, :], oh, "l_lines", ml, q=pool, eng=nc.gpsimd)

        spawn(bias_lines())

        rope_last = []

        def rope(nat, off, d, c0, out, *after):
            nh = nat.shape[2]
            if not rope_last:
                rope_last.append(ready["trig"])
            ra = RA[:, :, 0:nh * 2 * d].rearrange("p t (h e) -> p t h e", h=nh)
            rb = RB[:, :, 0:nh * 2 * d].rearrange("p t (h e) -> p t h e", h=nh)

            def tab(z, lo, n):
                return z[:, :, lo:lo + n].unsqueeze(2).to_broadcast([P, 2, nh, n])
            m1 = v_tt(ra, nat[:, :, :, off:off + 2 * d], tab(CS, c0, 2 * d), ALU.mult, after, rope_last)
            m2 = v_tt(rb[:, :, :, 0:d], nat[:, :, :, off + d:off + 2 * d], tab(SN, c0, d), ALU.mult, after, rope_last)
            m3 = v_tt(rb[:, :, :, d:2 * d], nat[:, :, :, off:off + d], tab(SN, c0 + d, d), ALU.mult, after, rope_last)
            m4 = v_tt(out, ra, rb, ALU.add, m1, m2, m3)
            rope_last[0] = m4
            return m4

        nat = Bufs([NAT[:, 0, :], NAT[:, 1, :]])
        for z in nat.idle:
            z.free = [m_nat0]

        def take_now(bufs):
            if not bufs.idle:
                force(lambda: bufs.idle)
            return bufs.take()

        ss_q, ss_kv = stat(2), stat(2)
        rs_q, rs_kv = stat(2), stat(2)
        rp_free = [None]

        def C_dst(k):
            return CTh[:, k, :], CTl[:, k, :]

        def evac_c(i, bk, m):
            n = (512, 320)[i]
            done("rs_x")
            nb = take_now(nat)
            nv = nb.ap.rearrange("p (t n) -> p t n", t=2)[:, :, 0:n]
            me = [a_copy(nv[:, t, :], bk[t].ap[:, 0:n], m, ready["rs_x"], nb.free, scale=rs_x[:, t:t + 1]) for t in range(2)]
            for t in range(2):
                main.give(bk[t], me[t])
            if i == 0:
                mq = [square(nv[:, t, :], ss_q[:, t:t + 1], me[t]) for t in range(2)]
                ready["rs_q"] = rstd_of(ss_q, 1, 512, rs_q, mq)
                spawn(to_parts("C", lambda k, t: nv[:, t, k * P:(k + 1) * P], me, C_dst, range(4),
                               GT[:, 112:118], after=lambda tr: nat.give(nb, tr, mq)))
                return
            mq = [square(nv[:, t, 0:256], ss_kv[:, t:t + 1], me[t]) for t in range(2)]
            ready["rs_kv"] = rstd_of(ss_kv, 1, 256, rs_kv, mq)

            def key_rope():
                while "trig" not in ready:
                    yield
                z = on_pool(lambda: nc.gpsimd.memset(KR[64:128, 0, :], 0.0))
                z2 = on_pool(lambda: nc.gpsimd.memset(KR[0:64, 1, :], 0.0))
                rp = RP[:, :, :].rearrange("p t (h e) -> p t h e", h=2)
                kin = nv[:, :, 256:320].unsqueeze(2)
                mr = rope(kin, 0, 32, 32, rp[:, :, 0:1, :], me, rp_free[0])
                mr2 = v_ts(rp[:, :, 1, :], rp[:, :, 0, :], 1.0, None, ALU.mult, None, mr)
                yield
                bb = yield from takes(side)
                mt = p_tr([(bb.ap[:, t * P:(t + 1) * P], RP[:, t, :]) for t in range(2)], mr2, bb.free)
                rp_free[0] = mt
                yield
                m1 = a_copy(KR[0:64, 0, :], bb.ap[0:64, 0:S], mt)
                m2 = a_copy(KR[64:128, 1, :], bb.ap[64:128, 0:S], mt)
                side.give(bb, m1, m2)
                ready["kr"] = [m1, m2, z, z2]
                kr_rope.append(mr)
                yield
            kr_rope = []
            gk = key_rope()
            spawn(gk)
            spawn(to_parts("C", lambda k, t: nv[:, t, k * P:(k + 1) * P], me, C_dst, range(4, 6),
                           GT[:, 112:118], after=lambda tr: ready.__setitem__("ckv_tr", tr)))

            def release():
                while "kr" not in ready or "ckv_tr" not in ready:
                    yield
                nat.give(nb, ready["ckv_tr"], mq, kr_rope)
            spawn(release())

        gemm_c = jc[0]
        cs0 = [s for s in gemm_c if s[0] == 0]
        cs1 = [s for s in gemm_c if s[0] == 1]
        gemm(cs0, KT, 512, from_T, evac_c)
        gemm(cs1, KT, 320, from_T, evac_c)

        def heads_to_T(name, nb, nv, me, dst, h0, nh, off, width, rope_args=None, extra=None):
            mr = me
            if rope_args:
                mr = [rope(nv, *rope_args, nv[:, :, :, rope_args[0]:rope_args[0] + 2 * rope_args[1]], me), me]
                yield
            trs, outs = [], []
            for h in range(0, nh, 2):
                bb = yield from takes(side)
                mt = p_tr([(bb.ap[:, hh * S + t * P:hh * S + (t + 1) * P], nv[:, t, h + hh, off:off + P])
                           for hh in range(2) for t in range(2)], mr, bb.free)
                trs.append(mt)
                outs.append((h, bb, mt))
            if nb is not None:
                nat.give(nb, trs)
            yield
            for h, bb, mt in outs:
                mo = a_copy(dst[:, h0 + h:h0 + h + 2, :], bb.ap.rearrange("p (h s) -> p h s", h=2), mt)
                side.give(bb, mo)
                for hh in range(2):
                    ready[(name, h0 + h + hh)] = mo

        def evac_qkv(i, bk, m):
            if i < 4:
                nb = take_now(nat)
                nv = nb.ap.rearrange("p (t n) -> p t n", t=2)
                me = [a_copy(nv[:, t, :], bk[t].ap, m, ready["rs_x"], nb.free, scale=rs_x[:, t:t + 1]) for t in range(2)]
                dst, nm = ((QT, "q"), (KTt, "k"))[i // 2]
                spawn(heads_to_T(nm, nb, nv.rearrange("p t (h e) -> p t h e", h=4), me, dst, 4 * (i % 2), 4, 0, P,
                                 (0, 16, 0)))
            else:
                me = [a_copy(V[:, t, 512 * (i - 4):512 * (i - 3)], bk[t].ap, m, ready["rs_x"], scale=rs_x[:, t:t + 1])
                      for t in range(2)]
                for h in range(4):
                    ready[("v", 4 * (i - 4) + h)] = me
            for t in range(2):
                main.give(bk[t], me[t])

        gemm(jqkv, KT, 512, from_T, evac_qkv)

        sbufs = Bufs([S1[:, i, :] for i in range(4)])
        ptbufs = Bufs([PT1[:, i, :] for i in range(2)])
        stats = Bufs([AS[:, i, :] for i in range(6)])
        alive = [0]
        for z in sbufs.idle:
            z.free = [done("lines")]

        def head(tag, h, scale, rope_part, y):
            alive[0] += 1
            m_q, m_k, m_v = ([done_now(x) for x in ((tag + "q", h), (tag + "k", h), (tag + "v", h))])
            deps = [m_q, m_k]
            if rope_part:
                deps += [done_now(("mqr", h)), ready["kr"]]
            bb = yield from takes(side)
            mms = []
            for t, (o, n) in enumerate(((0, P), (P, S))):
                ts = slice(t * P, (t + 1) * P)
                out = bb.ap[:, o:o + n]
                mms.append((out, QT[:, h, ts], KTt[:, h, 0:n], True, not rope_part))
                if rope_part:
                    mms.append((out, QR[:, h // 2, ts], KR[:, h % 2, 0:n], False, True))
            m1 = p_mm(mms, deps, bb.free)
            yield
            sbuf = yield from takes(sbufs)
            st = yield from takes(stats)
            s, a = sbuf.ap, st.ap
            m2 = v_stt(s, bb.ap[:, 0:384], scale, mask[:, :], ALU.mult, ALU.add, m1, m_mask, sbuf.free)
            side.give(bb, m2)
            m3 = v_max(a[:, 0:1], s[:, 0:P], m2, st.free)
            m4 = v_max(a[:, 1:2], s[:, P:384], m2, st.free)
            m5 = v_ts(a[:, 2:4], a[:, 0:2], -1.0, None, ALU.mult, None, m3, m4)
            yield
            m6 = [a_fn(ACT.Exp, s[:, lo:hi], s[:, lo:hi], m5, bias=a[:, 2 + t:3 + t], acc=a[:, 4 + t:5 + t])
                  for t, (lo, hi) in enumerate(((0, P), (P, 384)))]
            yield
            m7 = dve.do(lambda: nc.vector.reciprocal(a[:, 6:8], a[:, 4:6]), m6)
            m8 = [v_ts(s[:, lo:hi], s[:, lo:hi], a[:, 6 + t:7 + t], None, ALU.mult, None, m7)
                  for t, (lo, hi) in enumerate(((0, P), (P, 384)))]
            stats.give(st, m8)
            yield
            bb = yield from takes(side)
            m9 = p_tr([(bb.ap[:, i * P:(i + 1) * P], s[:, i * P:(i + 1) * P]) for i in range(3)], m8, bb.free)
            sbufs.give(sbuf, m9)
            yield
            pt = yield from takes(ptbufs)
            m10 = a_copy(pt.ap, bb.ap[:, 0:384], m9, pt.free)
            side.give(bb, m10)
            yield
            bb = yield from takes(side)
            hs = slice(h * P, (h + 1) * P)
            m11 = p_mm([(bb.ap[:, 0:S], V[:, 0, hs], pt.ap[:, 0:S], True, False),
                        (bb.ap[:, P:S], V[:, 1, hs], pt.ap[:, S:384], False, True)], m10, m_v, bb.free)
            ptbufs.give(pt, m11)
            yield
            m12 = a_copy(YF[:, y + h, :], bb.ap[:, 0:S], m11)
            side.give(bb, m12)
            ready[("y", y + h)] = m12
            alive[0] -= 1

        def done_now(key):
            return ready[key]

        def heads(tag, scale, rope_part, y, at_once):
            for h in range(8):
                keys = [(tag + "q", h), (tag + "k", h), (tag + "v", h)] + ([("mqr", h), "kr"] if rope_part else [])
                while alive[0] >= at_once or any(k not in ready for k in keys):
                    yield
                spawn(head(tag, h, scale, rope_part, y))
                yield

        spawn(heads("", P ** -0.5, False, 0, 3))

        def evac_gate(i, bk, m, base=0):
            n, ab = divmod(base + i, 2)
            me = [a_copy(G[:, n, ab, 0, :], bk[0].ap, m, ready["rs_x"], scale=rs_x[:, 0:1]),
                  v_ts(G[:, n, ab, 1, :], bk[1].ap, rs_x[:, 1:2], None, ALU.mult, None, m, ready["rs_x"])]
            for t in range(2):
                main.give(bk[t], me[t])
            ready[("g", n, ab)] = me

        gemm(jg1, KT, 512, from_T, evac_gate)
        force(lambda: all(("y", h) in ready for h in range(8)))

        def from_C(k0):
            def left(k):
                m = done(("C", k0 + k))
                return CTh[:, k0 + k, :], CTl[:, k0 + k, :], m
            return left

        done("rs_q")
        done("kr")

        def evac_uq(i, bk, m):
            nb = take_now(nat)
            nv = nb.ap.rearrange("p (t n) -> p t n", t=2)[:, :, 0:384]
            me = [a_copy(nv[:, 0, :], bk[0].ap[:, 0:384], m, ready["rs_q"], nb.free, scale=rs_q[:, 0:1]),
                  v_ts(nv[:, 1, :], bk[1].ap[:, 0:384], rs_q[:, 1:2], None, ALU.mult, None, m, ready["rs_q"], nb.free)]
            for t in range(2):
                main.give(bk[t], me[t])
            n4_ = nv.rearrange("p t (h e) -> p t h e", h=2)

            def go():
                mr = rope(n4_, P, 32, 32, RP[:, :, :].rearrange("p t (h e) -> p t h e", h=2), me, rp_free[0])
                yield
                bb = yield from takes(side)
                mt = p_tr([(bb.ap[:, hh * S + t * P:hh * S + (t + 1) * P], n4_[:, t, hh, 0:P])
                           for hh in range(2) for t in range(2)], me, bb.free)
                b2 = yield from takes(side)
                mt2 = p_tr([(b2.ap[:, t * P:(t + 1) * P], RP[:, t, :]) for t in range(2)], mr, b2.free)
                rp_free[0] = mt2
                nat.give(nb, mt, mr)
                yield
                mo = a_copy(QT[:, 2 * i:2 * i + 2, :], bb.ap.rearrange("p (h s) -> p h s", h=2), mt)
                side.give(bb, mo)
                m2 = a_copy(QR[:, i, :], b2.ap[:, 0:S], mt2)
                side.give(b2, m2)
                for hh in range(2):
                    ready[("mq", 2 * i + hh)] = mo
                    ready[("mqr", 2 * i + hh)] = m2
            spawn(go())

        gemm(juq, 4, 384, from_C(0), evac_uq)
        done("rs_kv")

        def evac_ukv(i, bk, m):
            nb = take_now(nat)
            nv = nb.ap.rearrange("p (t n) -> p t n", t=2)[:, :, 0:S]
            me, mv = [], []
            for t in range(2):
                src = bk[t].ap.rearrange("p (h n) -> p h n", h=2)
                ko = nv[:, t, :].rearrange("p (h e) -> p h e", h=2)
                vo = V[:, t, 2 * i * P:(2 * i + 2) * P].rearrange("p (h e) -> p h e", h=2)
                if t == 0:
                    me.append(a_copy(ko, src[:, :, 0:P], m, ready["rs_kv"], nb.free, scale=rs_kv[:, t:t + 1]))
                    mv.append(a_copy(vo, src[:, :, P:S], m, scale=rs_kv[:, t:t + 1]))
                else:
                    me.append(v_ts(ko, src[:, :, 0:P], rs_kv[:, t:t + 1], None, ALU.mult, None, m, ready["rs_kv"], nb.free))
                    mv.append(v_ts(vo, src[:, :, P:S], rs_kv[:, t:t + 1], None, ALU.mult, None, m))
                main.give(bk[t], me[t], mv[t])
            for hh in range(2):
                ready[("mv", 2 * i + hh)] = mv
            spawn(heads_to_T("mk", nb, nv.rearrange("p t (h e) -> p t h e", h=2), me, KTt, 2 * i, 2, 0, P))

        gemm(jukv, 2, 512, from_C(4), evac_ukv)
        spawn(heads("m", (P + 64) ** -0.5, True, 8, 3))
        m_xT = gemm(jg2, KT, 512, from_T, lambda i, bk, m: evac_gate(i, bk, m, 4))

        def split_y(h, m_free):
            mh = a_copy(Th[:, h, :], YF[:, h, :], done(("y", h)), m_free)
            ml = v_tt(Tl[:, h, :], YF[:, h, :], r32(Th[:, h, :]), ALU.subtract, mh, m_free)
            ready[("Y", h)] = [mh, ml]

        def split_all():
            for h in range(16):
                while ("y", h) not in ready:
                    yield
                split_y(h, m_xT)
                if h % 4 == 3:
                    yield
        spawn(split_all())

        def from_Y(h0):
            def left(k):
                m = done(("Y", h0 + k))
                return Th[:, h0 + k, :], Tl[:, h0 + k, :], m
            return left

        part = {}

        def branch_evac(n, ab):
            def evac(i, bk, m):
                g = G[:, n, ab, :, :]
                mg = a_fn(ACT.Sigmoid, g, g, ready[("g", n, ab)])
                me = [v_tt(g[:, t, :], bk[t].ap, g[:, t, :], ALU.mult, m, mg) for t in range(2)]
                for t in range(2):
                    main.give(bk[t], me[t])
                if ab == 0:
                    part[n] = me
                    return
                ga = G[:, n, 0, :, :]
                mm = v_tt(ga, ga, g, ALU.add, me, part[n])

                def dst(k):
                    return MT[:, n, 0, k, :], MT[:, n, 1, k, :]
                spawn(to_parts(("M", n), lambda k, t: G[:, n, 0, t, k * P:(k + 1) * P], mm, dst, range(4), None))
            return evac

        for n in range(4):
            gemm(jbr[n][0], 8, 512, from_Y(0), branch_evac(n, 0))
            gemm(jbr[n][1], 8, 512, from_Y(8), branch_evac(n, 1))
        m_yT = used[-1]

        def from_M(k):
            n, kk = divmod(k, 4)
            m = done((("M", n), kk))
            return MT[:, n, 0, kk, :], MT[:, n, 1, kk, :], m

        def residual(name_gain, ss_, out_marks, m_free):
            def evac(i, bk, m):
                cs_ = slice(512 * i, 512 * (i + 1))
                me = [v_tt(X[:, t, cs_], bk[t].ap, X[:, t, cs_], ALU.add, m) for t in range(2)]
                for t in range(2):
                    main.give(bk[t], me[t])
                    out_marks.append(square(X[:, t, cs_], ss_[:, 4 * t + i:4 * t + i + 1], me[t]))
                for k in range(4 * i, 4 * i + 4):
                    ready.pop(("T", k), None)
                spawn(to_parts("T", lambda k, t: X[:, t, (4 * i + k) * P:(4 * i + k + 1) * P], me,
                               T_dst, range(4 * i, 4 * i + 4), name_gain, free=m_free,
                               after=lambda tr: x_read.extend(tr)))
            return evac

        x_read = []
        ss2 = stat(8)
        rs2 = stat(2)
        m_ss2 = []
        for k in range(KT):
            ready.pop(("T", k), None)
        gemm(jout, KT, 512, from_M, residual(GT[:, 16:32], ss2, m_ss2, m_yT))
        m_rs2 = rstd_of(ss2, 4, D, rs2, m_ss2)

        sg_buf = Bufs([SG[:, :, :]])
        hid_buf = Bufs([HID[:, i, :, :] for i in range(2)])
        sg_now = {}

        def evac_gate1(i, bk, m):
            z = take_now(sg_buf)
            me = [a_fn(ACT.Silu, z.ap[:, t, :], bk[t].ap, m, m_rs2, z.free, scale=rs2[:, t:t + 1]) for t in range(2)]
            for t in range(2):
                main.give(bk[t], me[t])
            sg_now[0] = (z, me)

        def H_dst(k):
            return Hh[:, k, :], Hl[:, k, :]

        def evac_up1(f):
            def evac(i, bk, m):
                z, mg = sg_now[0]
                hb = take_now(hid_buf)
                me = [v_stt(hb.ap[:, t, :], bk[t].ap, rs2[:, t:t + 1], z.ap[:, t, :], ALU.mult, ALU.mult,
                            m, mg, hb.free) for t in range(2)]
                for t in range(2):
                    main.give(bk[t], me[t])
                sg_buf.give(z, me)
                spawn(to_parts("H", lambda k, t: hb.ap[:, t, k * P:(k + 1) * P], me, H_dst,
                               range(4 * f, 4 * f + 4), None, after=lambda tr: hid_buf.give(hb, tr)))
            return evac

        for f in range(NF):
            gemm(jff[f][0], KT, 512, from_T, evac_gate1)
            gemm(jff[f][1], KT, 512, from_T, evac_up1(f))
        m_ff = used[-1]

        def from_H(k):
            m = done(("H", k))
            return Hh[:, k, :], Hl[:, k, :], m

        ss3, rs3 = stat(8), stat(2)
        m_ss3 = []
        x_read.clear()
        gb_v = bass.AP(A["final_norm"].tensor, 0, [[0, P], [1, D]])
        m_gf = load(GB[:, :], gb_v, "l_gf", [z.free for z in nat.idle], q=pool, eng=nc.gpsimd)
        m_down = gemm(jdown, FT, 512, from_H, residual(GFN[:, :], ss3, m_ss3, [m_ff, m_gfn]))
        m_rs3 = rstd_of(ss3, 4, D, rs3, m_ss3)

        ss4, rs4, rs34 = stat(8), stat(2), stat(2)

        def norm_between():
            while any(("T", k) not in ready for k in range(KT)):
                yield
            marks = []
            for c in range(4):
                for t in range(2):
                    xs = X[:, t, 512 * c:512 * (c + 1)]
                    mx = v_stt(xs, xs, rs3[:, t:t + 1], GB[:, 512 * c:512 * (c + 1)], ALU.mult, ALU.mult,
                               m_rs3, m_gf, x_read)
                    marks.append(square(xs, ss4[:, 4 * t + c:4 * t + c + 1], mx))
                    ready[("xb", c, t)] = mx
                yield
            mr = rstd_of(ss4, 4, D, rs4, marks)
            ready["rs34"] = v_tt(rs34, rs3, rs4, ALU.mult, mr, m_rs3)
            ready["gb"] = [ready[("xb", c, t)] for c in range(4) for t in range(2)]
        spawn(norm_between())

        m_kz = [on_pool(lambda: nc.gpsimd.memset(KK[64:128, :, 0, :], 0.0), m_down),
                on_pool(lambda: nc.gpsimd.memset(KK[0:64, :, 1, :], 0.0), m_down)]
        l_bt = [lane("l_bt0"), lane("l_bt1")]
        bt = {}

        def load_bias(c, *after):
            src = bass.AP(lines, 8 * c * 384, [[1, P], [384, 8], [1, S]])
            bt[c] = pool.dma(BT[:, c % 2, :, :], src, l_bt[c % 2], after, eng=nc.gpsimd)

        for c in range(2):
            load_bias(c, m_down, done("lines"))

        def bt_view(c, e, n):
            base = BT[:, c % 2, 2 * e:2 * e + 2, 0:n]
            pat = [list(z) for z in base.ap]
            pat[-1] = [-1, n]
            return bass.AP(base.tensor, base.offset + n - 1, pat)

        pairs = {"n": 0, "bt": {0: [], 1: [], 2: [], 3: []}}
        sb2 = Bufs([S2a[:, 0, :], S2a[:, 1, :], S2b[:, 0, :], S2b[:, 1, :]])
        pt2 = Bufs([PT2[:, 0, :], PT2[:, 1, :]])
        for z in sb2.idle + pt2.idle:
            z.free = [m_down]
        qp = Bufs([QP[:, 0, :, :], QP[:, 1, :, :]])

        def pair(c, e, qb):
            j = 4 * c + e
            g = j // 2
            st = yield from takes(stats)
            a = st.ap
            b0 = yield from takes(side)
            b1 = yield from takes(side)
            m1 = p_mm([(b0.ap[:, 0:S], qb.ap[:, e, 0:P], KK[:, g, :, 0:P], True, True)],
                      ready[("q2", c)], ready[("k2", g)], b0.free)
            m1b = p_mm([(b1.ap, qb.ap[:, e, P:S], KK[:, g, :, :].rearrange("p a s -> p (a s)"), True, True)], b1.free)
            pairs[("qp", c)].append(m1b)
            if len(pairs[("qp", c)]) == 4:
                qp.give(qb, pairs[("qp", c)])
            yield
            sbuf = yield from takes(sb2)
            s = sbuf.ap
            m2 = v_stt(s[:, 0:S].rearrange("p (h n) -> p h n", h=2), b0.ap[:, 0:S].rearrange("p (h n) -> p h n", h=2),
                       0.125, bt_view(c, e, P), ALU.mult, ALU.add, m1, bt[c], sbuf.free)
            side.give(b0, m2)
            m3 = v_stt(s[:, S:768].rearrange("p (h n) -> p h n", h=2), b1.ap.rearrange("p (h n) -> p h n", h=2),
                       0.125, bt_view(c, e, S), ALU.mult, ALU.add, m1b, bt[c], sbuf.free)
            side.give(b1, m3)
            pairs["bt"][c] += [m2, m3]
            if len(pairs["bt"][c]) == 8 and c < 2:
                load_bias(c + 2, pairs["bt"][c])
            m4 = v_max(a[:, 0:2], s[:, 0:S].rearrange("p (h n) -> p h n", h=2), m2, st.free)
            m5 = v_max(a[:, 2:4], s[:, S:768].rearrange("p (h n) -> p h n", h=2), m3, st.free)
            av = a[:, 0:4].rearrange("p (t h) -> p t h", t=2)
            dv = a[:, 4:8].rearrange("p (t h) -> p t h", t=2)
            sk = SK[:, 2 * j:2 * j + 2].unsqueeze(1).to_broadcast([P, 2, 2])
            m6 = v_tt(av, av, sk, ALU.max, m4, m5, m_sk)
            m7 = v_tt(dv, sk, av, ALU.subtract, m6)
            m8 = v_ts(a[:, 0:4], a[:, 0:4], -1.0, None, ALU.mult, None, m6, m7)
            yield
            parts = ((0, 128), (128, 256), (256, 512), (512, 768))
            m9 = [a_fn(ACT.Exp, s[:, lo:hi], s[:, lo:hi], m8, bias=a[:, i:i + 1], acc=a[:, 8 + i:9 + i])
                  for i, (lo, hi) in enumerate(parts)]
            m9.append(a_fn(ACT.Exp, a[:, 4:8], a[:, 4:8], m7))
            yield
            m10 = v_tt(a[:, 8:12], a[:, 8:12], a[:, 4:8], ALU.add, m9)
            m11 = dve.do(lambda: nc.vector.reciprocal(a[:, 12:16], a[:, 8:12]), m10)
            m12 = [v_ts(s[:, lo:hi], s[:, lo:hi], a[:, 12 + i:13 + i], None, ALU.mult, None, m11)
                   for i, (lo, hi) in enumerate(parts)]
            stats.give(st, m12)
            yield
            c0 = yield from takes(side)
            c1 = yield from takes(side)
            m13 = p_tr([(c0.ap[:, i * P:(i + 1) * P], s[:, o:o + P]) for i, o in enumerate((0, 256, 128, 512))],
                       m12, c0.free)
            m14 = p_tr([(c1.ap[:, i * P:(i + 1) * P], s[:, o:o + P]) for i, o in enumerate((384, 640))], c1.free)
            sb2.give(sbuf, m14)
            yield
            pt = yield from takes(pt2)
            m15 = a_copy(pt.ap[:, 0:512], c0.ap, m13, pt.free)
            m16 = v_ts(pt.ap[:, 512:768], c1.ap[:, 0:S], 1.0, None, ALU.mult, None, m14, pt.free)
            side.give(c0, m15)
            side.give(c1, m16)
            yield
            o = yield from takes(side)
            kts = o.ap.rearrange("p (h n) -> p h n", h=2)[:, :, P:S]
            m17 = p_mm([(o.ap, VV[:, 0, g, :, :].rearrange("p a e -> p (a e)"), pt.ap[:, 0:512], True, False),
                        (kts, VV[:, 1, g, :, :].rearrange("p a e -> p (a e)"), pt.ap[:, 512:768].rearrange(
                            "p (h n) -> p h n", h=2), False, True)], m15, m16, ready["v2"], o.free)
            pt2.give(pt, m17)
            yield
            mh = [a_copy(YH[64 * z:64 * z + 64, j, :], o.ap[64 * z:64 * z + 64, S * z:S * z + S], m17)
                  for z in range(2)]
            ml = [v_tt(YL[64 * z:64 * z + 64, j, :], o.ap[64 * z:64 * z + 64, S * z:S * z + S],
                       r32(YH[64 * z:64 * z + 64, j, :]), ALU.subtract, mh) for z in range(2)]
            side.give(o, ml)
            ready[("Y2", j)] = [mh, ml]
            pairs["n"] -= 1

        def evac_in2(i, bk, m):
            if i == 0:
                rs = done("rs34")
                nbs = []
                nats = [take_now(nat), take_now(nat)]
                for t in range(2):
                    nv = nats[t].ap.rearrange("p (g a e) -> p g a e", g=8, a=2)
                    src = bk[t].ap.rearrange("p (g e) -> p g e", g=8)
                    ma = a_copy(nv[:, :, 0, :], src, m, rs, nats[t].free, ready["gb"], scale=rs34[:, t:t + 1])
                    mb = v_ts(nv[:, :, 1, :], src, rs34[:, t:t + 1], None, ALU.mult, None, ma, nats[t].free, ready["gb"])
                    main.give(bk[t], ma, mb)
                    nbs.append((nv, [ma, mb]))

                def go():
                    trs = []
                    for g in range(0, 8, 2):
                        bb = yield from takes(side)
                        mt = p_tr([(bb.ap[:, gg * S + t * P:gg * S + (t + 1) * P],
                                    nbs[t][0][:, g + gg, :, :].rearrange("p a e -> p (a e)"))
                                   for gg in range(2) for t in range(2)], nbs[0][1], nbs[1][1], bb.free)
                        trs.append(mt)
                        yield
                        bv = bb.ap.rearrange("p (g s) -> p g s", g=2)
                        mo = [a_copy(KK[64 * z:64 * z + 64, g:g + 2, z, :], bv[64 * z:64 * z + 64], mt, m_kz)
                              for z in range(2)]
                        side.give(bb, mo)
                        ready[("k2", g)] = ready[("k2", g + 1)] = [mo, m_kz]
                    for z in nats:
                        nat.give(z, trs)
                spawn(go())
                return
            if i == 1:
                mv = []
                for t in range(2):
                    src = bk[t].ap.rearrange("p (g e) -> p g e", g=8)
                    ma = a_copy(VV[:, t, :, 0, :], src, m, scale=rs34[:, t:t + 1])
                    mb = v_ts(VV[:, t, :, 1, :], src, rs34[:, t:t + 1], None, ALU.mult, None, ma)
                    main.give(bk[t], ma, mb)
                    mv += [ma, mb]
                ready["v2"] = mv
                return
            c = i - 2
            nb = take_now(nat)
            nv = nb.ap.rearrange("p (t n) -> p t n", t=2)
            me = [a_copy(nv[:, t, :], bk[t].ap, m, nb.free, scale=rs34[:, t:t + 1]) for t in range(2)]
            for t in range(2):
                main.give(bk[t], me[t])
            pairs[("qp", c)] = []

            def go():
                qb = yield from takes(qp)
                held, trs = [], []
                for e in range(0, 4, 2):
                    bb = yield from takes(side)
                    mt = p_tr([(bb.ap[:, ee * S + t * P:ee * S + (t + 1) * P], nv[:, t, (e + ee) * P:(e + ee + 1) * P])
                               for ee in range(2) for t in range(2)], me, bb.free)
                    held.append((e, bb, mt))
                    trs.append(mt)
                nat.give(nb, trs)
                nat_last[c] = trs
                yield
                mo = []
                for e, bb, mt in held:
                    mo.append(a_copy(qb.ap[:, e:e + 2, :], bb.ap.rearrange("p (h s) -> p h s", h=2), mt, qb.free))
                    side.give(bb, mo[-1])
                ready[("q2", c)] = mo
                yield
                for e in range(4):
                    while pairs["n"] >= 4:
                        yield
                    pairs["n"] += 1
                    spawn(pair(c, e, qb))
                    yield
            spawn(go())

        nat_last = {}
        gemm(jin2, KT, 512, from_T, evac_in2)
        m_T2 = used[-1]
        force(lambda: 3 in nat_last)
        m_g1 = load(GB[:, :], bass.AP(A["norm_g_2"].tensor, D, [[0, P], [1, D]]), "l_g1",
                    list(nat_last.values()), q=pool, eng=nc.gpsimd)

        def from_Y2(k):
            m = done(("Y2", k))
            return YH[:, k, :], YL[:, k, :], m

        def evac_post(dst, gb, m_gb, ss_, marks, m_free):
            def evac(i, bk, m):
                cs_ = slice(512 * i, 512 * (i + 1))
                for t in range(2):
                    mq = square(bk[t].ap, ss_[:, 4 * t + i:4 * t + i + 1], m)
                    mg = v_tt(dst[:, t, cs_], bk[t].ap, gb[:, cs_], ALU.mult, mq, m_gb, m_free)
                    main.give(bk[t], mg)
                    marks[(i, t)] = (mq, mg)
            return evac

        ss5, rs5, ss6, rs6 = stat(8), stat(2), stat(8), stat(2)
        mk5 = {}
        force(lambda: not tasks or all(("Y2", k) in ready for k in range(split_at)))
        gemm(jout2, KT, 512, from_Y2, evac_post(MG, GB, m_g1, ss5, mk5, None))
        m_out2 = used[-1]
        m_rs5 = rstd_of(ss5, 4, D, rs5, [v[0] for v in mk5.values()])
        for k in range(KT):
            ready.pop(("T", k), None)
        m_ss6 = []
        x_read.clear()
        for c in range(4):
            me = []
            for t in range(2):
                xs = slice(512 * c, 512 * (c + 1))
                me.append(v_stt(X[:, t, xs], MG[:, t, xs], rs5[:, t:t + 1], X[:, t, xs], ALU.mult, ALU.add,
                                m_rs5, mk5[(c, t)][1], ready[("xb", c, t)]))
            spawn(to_parts("T", lambda k, t, c=c: X[:, t, (4 * c + k) * P:(4 * c + k + 1) * P], me,
                           T_dst, range(4 * c, 4 * c + 4), GT[:, 80:96], free=m_T2), 0)
            pump()
            m_ss6 += [square(X[:, t, xs], ss6[:, 4 * t + c:4 * t + c + 1], me[t]) for t in range(2)]
        m_rs6 = rstd_of(ss6, 4, D, rs6, m_ss6)
        done(("T", 3))

        R = RP[:, :, :].rearrange("p t s -> p (t s)")

        def row_factor():
            m1 = dve.do(lambda: nc.vector.memset(RB[:, 0, :], 1.0))
            m2 = [v_ts(RA[:, t, :], ident[:, :], rs6[:, t:t + 1], None, ALU.mult, None, m_rs6) for t in range(2)]
            yield
            bb = yield from takes(side)
            m3 = p_mm([(bb.ap[:, t * P:(t + 1) * P], RB[:, 0, :], RA[:, t, :], True, True) for t in range(2)],
                      m1, m2, bb.free)
            yield
            m4 = a_copy(R, bb.ap[:, 0:S], m3)
            side.give(bb, m4)
            ready["R"] = m4
        spawn(row_factor())

        m_uz = [dve.do(lambda: nc.vector.memset(U[:, :, 0:2], 0.0), m_out2)]
        ub = Bufs([U[:, i, :] for i in range(4)])
        cb = Bufs([C[:, i, :] for i in range(3)])
        sg2_free = {}
        sg2_now = {}
        m_g3 = load(GB[:, :], bass.AP(A["norm_g_2"].tensor, 3 * D, [[0, P], [1, D]]), "l_g3",
                    [v[1] for v in mk5.values()], q=pool, eng=nc.gpsimd)

        def conv(bank, m, ft, f, gate):
            u = yield from takes(ub)
            cc = yield from takes(cb)
            m1 = v_tt(u.ap[:, 2:258], bank.ap[:, 0:S], R, ALU.mult, m, ready["R"], u.free, m_uz)
            both.give(bank, m1)
            m2 = v_ts(cc.ap, u.ap[:, 0:S], CW[:, 0, ft:ft + 1], None, ALU.mult, None, m1, cc.free)
            m3 = v_stt(cc.ap, u.ap[:, 1:257], CW[:, 1, ft:ft + 1], cc.ap, ALU.mult, ALU.add, m2)
            m4 = v_stt(cc.ap, u.ap[:, 2:258], CW[:, 2, ft:ft + 1], cc.ap, ALU.mult, ALU.add, m3)
            ub.give(u, m4)
            if gate:
                yield
                m5 = a_fn(ACT.Silu, SG2[:, f, :], cc.ap, m4, sg2_free.get(f))
                cb.give(cc, m5)
                sg2_now[(ft // 4, f)] = m5
                return
            k = ft - FT
            m5 = v_tt(cc.ap, cc.ap, SG2[:, f, :], ALU.mult, m4, sg2_now[(k // 4, f)])
            sg2_free[f] = m5
            yield
            m6 = a_copy(Hh[:, k, :], cc.ap, m5)
            yield
            m7 = v_tt(Hl[:, k, :], cc.ap, r32(Hh[:, k, :]), ALU.subtract, m6)
            cb.give(cc, m7)
            ready[("H2", k)] = [m6, m7]

        both = Bufs([])

        def gemm_t(steps, f0, gate):
            bk = [take_now(both) for _ in range(4)]
            for _, k0, a in steps:
                hi, lo, m_w = chunk()
                for kk in range(a):
                    k = k0 + kk
                    th, tl, m_l = from_T(k)
                    mms = []
                    for f in range(4):
                        o, fs = bk[f].ap[:, 0:S], slice(f * P, (f + 1) * P)
                        mms += [(o, hi[:, kk, fs], th, k == 0, False),
                                (o, hi[:, kk, fs], tl, False, False),
                                (o, lo[:, kk, fs], th, False, k == KT - 1)]
                    m = p_mm(mms, m_w, m_l, [z.free for z in bk] if k == 0 else None)
                used.append(m)
                if k0 + a == KT:
                    if "R" not in ready:
                        done("R")
                    for f in range(4):
                        spawn(conv(bk[f], m, f0 + f, f, gate), 2 * f)
                if len(side.idle) == 4 and "R" in ready and all(("T", z) in ready for z in range(KT)):
                    both.idle, side.idle = both.idle + side.idle, []
                pump()

        both.idle, main.idle = main.idle, []
        for f in range(NF):
            gemm_t(jff2[f][0], 4 * f, True)
            gemm_t(jff2[f][1], FT + 4 * f, False)
        m_T3 = used[-1]
        main = both

        def from_H2(k):
            m = done(("H2", k))
            return Hh[:, k, :], Hl[:, k, :], m

        ss7, rs7 = stat(8), stat(2)
        mk7 = {}
        gemm(jdown2, FT, 512, from_H2, evac_post(MG2, GB, m_g3, ss7, mk7, m_T3))
        m_rs7 = rstd_of(ss7, 4, D, rs7, [v[0] for v in mk7.values()])
        out_v = A["out"].rearrange("b (t p) d -> p (b t) d", p=P)
        for c in range(4):
            xs = slice(512 * c, 512 * (c + 1))
            me = [v_stt(X[:, t, xs], MG2[:, t, xs], rs7[:, t:t + 1], X[:, t, xs], ALU.mult, ALU.add,
                        m_rs7, mk7[(c, t)][1]) for t in range(2)]
            last = sp.dma(out_v[:, :, xs], X[:, :, xs], l_out, me, eng=nc.sync)
        assert at_job["use"] == len(jobs) and not tasks

        for q in (pe, act, dve, pool):
            q.number()
        block = ctx.enter_context(nc.Block())

        @block.sync
        def _(eng):
            sp.emit(eng)
            eng.wait_ge(last.sem, last.value)

        @block.gpsimd
        def _(eng):
            pool.emit(eng)
            eng.wait_ge(ready["lines"].sem, ready["lines"].value)

        @block.scalar
        def _(eng):
            act.emit(eng)

        @block.vector
        def _(eng):
            dve.emit(eng)

        @block.tensor
        def _(eng):
            pe.emit(eng)


def constants():
    f = np.float32
    c = np.zeros((P, 560), f)
    c[:, 0:128] = np.eye(P, dtype=f)
    tri = np.where(np.arange(P)[None, :] <= np.arange(P)[:, None], 0.0, NEG).astype(f)
    c[:, 128:256] = tri
    c[:, 384:512] = tri
    for o, d in ((512, 32), (528, 64)):
        fr = f(500000.0) ** (-np.arange(0, d, 2, dtype=f) / f(d))
        c[:, o:o + d // 2] = fr.astype(f)[None, :]
    b = np.zeros((32, 768), f)
    b[:, 384:768] = NEG
    for i in range(127, 255):
        n = i - 127
        if n < 16:
            k = n
        else:
            k = min(16 + int(f(math.log(n / 16) / math.log(8)) * f(16)), 31)
        b[k, i] = 1.0
        b[:, 384 + i] = 0.0
    return c, b


_INS = ["x", "positions", "attn_norm", "w_in", "q_norm", "w_uq", "kv_norm", "w_ukv", "w_branch_a", "w_branch_b",
        "w_out", "ffn_norm", "w_gate", "w_up", "w_down", "final_norm", "rel_bias_table_2", "norm_g_2",
        "ffn_w_up_2", "ffn_conv_2", "ffn_w_down_2", "swa_w_in_2", "swa_w_out_2", "swa_sinks_2"]


def kernel(**inputs):
    import numpy as _np
    import concourse.bacc as _bacc
    from concourse import mybir as _mybir
    from concourse.bass_utils import run_bass_kernel_spmd as _run

    nc = _bacc.Bacc("TRN2", target_bir_lowering=False, num_devices=1)
    c_main, c_bias = constants()
    arrays = {n: _np.ascontiguousarray(inputs[n]) for n in _INS}
    arrays["c_main"], arrays["c_bias"] = c_main, c_bias
    feed, args = {}, {}
    for name, a in arrays.items():
        feed[f"in_{name}_dram"] = a
        args[name] = nc.dram_tensor(f"in_{name}_dram", a.shape, _mybir.dt.from_np(a.dtype), kind="ExternalInput").ap()
    args["out"] = nc.dram_tensor("out_0_dram", (1, S, D), F32, kind="ExternalOutput").ap()
    build(nc, args)
    r = _run(nc, [feed], core_ids=[0])
    return r.results[0]["out_0_dram"]
```

```python
import math
from contextlib import ExitStack

import numpy as np

import concourse.bass as bass
from concourse import mybir

F32 = mybir.dt.float32
F32R = mybir.dt.float32r
BF16 = mybir.dt.bfloat16
I32 = mybir.dt.int32
ALU = mybir.AluOpType
ACT = mybir.ActivationFunctionType
AX = mybir.AxisListType.X

P = 128
D = 2048
S = 256
KT = D // P
IN = 8000
FF = 5632
NF = FF // 512
FT = FF // P
EPS = 1e-6
NEG = -1.0e30
RAW = 4
PAIR = 3
MAGIC = 12582912.0


class Mark:
    __slots__ = ("used", "sem", "value")

    def __init__(self, sem=None, value=None):
        self.used, self.sem, self.value = False, sem, value


class Queue:

    def __init__(self, sem):
        self.sem, self.items = sem, []

    def do(self, fn, *after):
        m = Mark()
        self.items.append((fn, flat(after), m, 1))
        return m

    def dma(self, out, src, lane, *after, eng, **how):
        lane[1] += 16
        m = Mark(lane[0], lane[1])
        self.items.append((lambda: eng.dma_start(out, src, **how), flat(after), m, 16))
        return m

    def number(self):
        n = 0
        for _, _, m, inc in self.items:
            if inc == 1 and m.used:
                n += 1
                m.sem, m.value = self.sem, n

    def emit(self, eng):
        seen = {}
        for fn, after, m, inc in self.items:
            need = {}
            for a in after:
                if a.value > need.get(a.sem.name, (0, None))[0]:
                    need[a.sem.name] = (a.value, a.sem)
            for name, (value, sem) in need.items():
                if seen.get(name, 0) < value:
                    seen[name] = value
                    eng.wait_ge(sem, value)
            ins = fn()
            if inc == 16 or m.used:
                ins.then_inc(m.sem, inc)


def flat(xs):
    out = []
    for x in xs:
        if x is None:
            continue
        if isinstance(x, Mark):
            x.used = True
            out.append(x)
        else:
            out += flat(x)
    return out


class Buf:

    def __init__(self, ap):
        self.ap, self.free = ap, []


class Bufs:
    def __init__(self, aps):
        self.idle = [Buf(a) for a in aps]

    def take(self):
        return self.idle.pop(0) if self.idle else None

    def give(self, b, *marks):
        b.free = list(marks)
        self.idle.append(b)


def build(nc, A):
    ctx = ExitStack()
    with ctx:
        def sb(name, shape, dt=F32):
            return ctx.enter_context(nc.sbuf_tensor(name, shape, dt))

        def region(name, floats):
            t = sb(name, [P, floats])
            return t, nc.sbuf_base - 4 * floats

        def at(name, reg, off, shape, dt=F32):
            return nc.alloc_sbuf_tensor_at(name, [P] + shape, dt, offset=reg + 4 * off)

        def sem(name):
            return ctx.enter_context(nc.semaphore(name))

        def lane(name):
            return [sem(name), 0]

        raw = sb("raw", [P, RAW, 1024])
        whi = sb("whi", [P, PAIR, 1024], F32R)
        wlo = sb("wlo", [P, PAIR, 1024], F32R)
        X = sb("X", [P, 2, D])
        _, rT = region("regT", 8192)
        _, rH = region("regH", 22528)
        _, rN = region("regN", 2048)
        _, rW = region("regW", 3072)
        TT = at("TT", rT, 0, [KT, 2, S], F32R)
        Th, Tl = TT[:, :, 0, :], TT[:, :, 1, :]
        G = at("G", rH, 0, [4, 2, 2, 512])
        MT = at("MT", rH, 0, [4, 2, 4, S], F32R)
        YF = at("YF", rH, 8192, [16, S])
        CTh = at("CTh", rH, 12288, [6, S], F32R)
        CTl = at("CTl", rH, 13824, [6, S], F32R)
        QT = at("QT", rH, 15360, [8, S])
        KTt = at("KTt", rH, 17408, [8, S])
        V = at("V", rH, 19456, [2, 1024])
        QR = at("QR", rH, 21504, [4, S])
        KR = at("KR", rW, 2304, [2, S])
        S1 = at("S1", rW, 0, [4, 384])
        PT1 = at("PT1", rW, 1536, [2, 384])
        Hh = at("Hh", rH, 0, [FT, S], F32R)
        Hl = at("Hl", rH, 11264, [FT, S], F32R)
        SG = at("SG", rW, 0, [2, 512])
        HID = at("HID", rW, 1024, [2, 2, 512])
        U = at("U", rW, 0, [4, 258])
        SG2 = at("SG2", rW, 1032, [4, S])
        C = at("C", rW, 2056, [3, S])
        KK = at("KK", rH, 0, [8, 2, S])
        MG = at("MG", rH, 0, [2, D])
        VV = at("VV", rH, 4096, [2, 8, 2, 64])
        QP = at("QP", rH, 6144, [2, 4, S])
        YH = at("YH", rH, 8192, [16, S], F32R)
        YL = at("YL", rH, 12288, [16, S], F32R)
        BT = at("BT", rH, 16384, [2, 8, S])
        S2a = at("S2a", rH, 20480, [2, 768])
        S2b = at("S2b", rW, 0, [2, 768])
        PT2 = at("PT2", rW, 1536, [2, 768])
        PR = at("PR", rT, 6144, [2, 2, 512])
        MG2 = at("MG2", rT, 0, [2, D])
        NAT = at("NAT", rN, 0, [2, 1024])
        GB = at("GB", rN, 0, [D])
        STG = at("STG", rN, 0, [4, P])
        ident = sb("ident", [P, P])
        mask = sb("mask", [P, 384])
        freq = sb("freq", [P, 48])
        CS = sb("CS", [P, 2, 96])
        SN = sb("SN", [P, 2, 96])
        GT = sb("GT", [P, 118])
        GFN = sb("GFN", [P, 16])
        CW = sb("CW", [P, 3, 88])
        SK = sb("SK", [P, 32])
        ST = sb("ST", [P, 144])
        AS = sb("AS", [P, 6, 16])
        JK = sb("JK", [P, 512], BF16)
        RA = sb("RA", [P, 2, P])
        RB = sb("RB", [P, 2, P])
        RP = sb("RP", [P, 2, P])
        PI = sb("PI", [P, 2], I32)

        banks = [ctx.enter_context(nc.psum_tensor(f"bank{i}", [P, 512], F32)) for i in range(8)]
        lines = nc.dram_tensor("bias_lines", [32, 384], F32)

        pe, act, dve, pool = (Queue(sem(f"s_{n}")) for n in ("pe", "act", "dve", "pool"))
        sp = Queue(None)
        l_raw = [lane(f"l_raw{i}") for i in range(RAW)]
        l_x = [lane(f"l_x{i}") for i in range(5)]
        l_out = lane("l_out")

        def load(out, src, name, *after, q=sp, eng=nc.sync, **how):
            return q.dma(out, src, lane(name), *after, eng=eng, **how)

        def a_copy(out, src, *after, scale=1.0):
            return act.do(lambda: nc.scalar.activation(out, src, ACT.Copy, scale=scale), *after)

        def a_fn(fn, out, src, *after, scale=1.0, bias=0.0, acc=None):
            if acc is None:
                return act.do(lambda: nc.scalar.activation(out, src, fn, bias=bias, scale=scale), *after)
            return act.do(lambda: nc.scalar.activation(out, src, fn, bias=bias, scale=scale, accum_out=acc), *after)

        def v_tt(out, a, b, op, *after):
            return dve.do(lambda: nc.vector.tensor_tensor(out, a, b, op), *after)

        def v_ts(out, a, s1, s2, op0, op1, *after):
            if s2 is None:
                return dve.do(lambda: nc.vector.tensor_scalar(out, a, s1, None, op0), *after)
            return dve.do(lambda: nc.vector.tensor_scalar(out, a, s1, s2, op0, op1), *after)

        def v_stt(out, a, s, b, op0, op1, *after):
            return dve.do(lambda: nc.vector.scalar_tensor_tensor(out=out, in0=a, scalar=s, in1=b, op0=op0, op1=op1), *after)

        def v_max(out, a, *after):
            return dve.do(lambda: nc.vector.reduce_max(out, a, AX), *after)

        def p_mm(list_, *after):
            def go():
                for out, lhsT, rhs, start, stop in list_:
                    last = nc.tensor.matmul(out, lhsT, rhs, start=start, stop=stop)
                return last
            return pe.do(go, *after)

        def p_tr(list_, *after):
            def go():
                for out, in_ in list_:
                    last = nc.tensor.transpose(out, in_, ident[:, :])
                return last
            return pe.do(go, *after, m_ident)

        pool_last = [None]

        def on_pool(fn, *after):
            pool_last[0] = pool.do(fn, after, pool_last[0])
            return pool_last[0]

        def r32(ap):
            return ap.bitcast(F32)

        main = Bufs([b[:, :] for b in banks[0:4]])
        side = Bufs([b[:, :] for b in banks[4:8]])

        tasks = []

        def later(g, n):
            for _ in range(n):
                yield
            yield from g

        def spawn(g, wait=1):
            tasks.append(later(g, wait) if wait else g)

        def pump():
            for g in list(tasks):
                if next(g, "end") == "end":
                    tasks.remove(g)

        def force(done):
            n = 0
            while not done():
                pump()
                n += 1
                assert n < 1000, "a task never ends"

        def takes(bufs):
            while True:
                b = bufs.take()
                if b is not None:
                    return b
                yield

        w = {n: A[n].rearrange("l (k p) n -> (l p) k n", p=P) for n in (
            "w_in", "w_uq", "w_ukv", "w_branch_a", "w_branch_b", "w_out", "w_gate", "w_up", "w_down",
            "swa_w_in_2", "swa_w_out_2", "ffn_w_up_2", "ffn_w_down_2")}
        jobs = []

        def product(name, groups, kt, order=None):
            steps = order or [(i, k, min(2, kt - k)) for i in range(len(groups)) for k in range(0, kt, 2)]
            for i, k, a in steps:
                c, n = groups[i]
                jobs.append((w[name][:, k:k + a, c:c + n], a, n))
            return steps

        jc = [product("w_in", [(3072, 512), (3584, 320)], KT)]
        jqkv = product("w_in", [(512 * i, 512) for i in range(6)], KT)
        gcols = [(3904 + D * ab + 512 * n, 512) for n in range(4) for ab in range(2)]
        jg1 = product("w_in", gcols[:4], KT)
        juq = product("w_uq", [(384 * i, 384) for i in range(4)], 4)
        jukv = product("w_ukv", [(512 * i, 512) for i in range(4)], 2)
        jg2 = product("w_in", gcols[4:], KT)
        n4 = [(512 * i, 512) for i in range(4)]
        jbr = []
        for i in range(4):
            jbr.append((product("w_branch_a", n4[i:i + 1], 8), product("w_branch_b", n4[i:i + 1], 8)))
        jout = product("w_out", n4, KT)
        jff = []
        for i in range(NF):
            c = [(512 * i, 512)]
            jff.append((product("w_gate", c, KT), product("w_up", c, KT)))
        jdown = product("w_down", n4, FT)
        icols = [(2048, 512), n4[0], (2560, 512)] + n4[1:]
        jin2 = product("swa_w_in_2", icols, KT)
        half = KT // 2
        orders = [[(i, k, 2) for i in (2, 3) for k in range(0, half, 2)],
                  [(i, k, 2) for k0, k1 in ((0, half), (half, 12), (12, 14), (14, KT)) for i in (0, 1)
                   for k in range(k0, k1, 2)],
                  [(i, k, 2) for i in (2, 3) for k in range(half, KT, 2)]]
        jout2 = [product("swa_w_out_2", n4, KT, o) for o in orders]
        jff2 = []
        for i in range(NF):
            jff2.append((product("ffn_w_up_2", [(512 * i, 512)], KT),
                         product("ffn_w_up_2", [(FF + 512 * i, 512)], KT)))
        jdown2 = product("ffn_w_down_2", n4, FT)

        at_job = {"fetch": 0, "split": 0, "use": 0}
        split_hi, split_lo, used = [], [], []

        def fetch():
            i = at_job["fetch"]
            if i >= len(jobs):
                return
            src, a, n = jobs[i]
            before = [split_hi[i - RAW], split_lo[i - RAW]] if i >= RAW else None
            out = raw[:, i % RAW, 0:a * n].rearrange("p (a n) -> p a n", a=a)
            fetched.append(sp.dma(out, src, l_raw[i % RAW], before, eng=nc.sync))
            at_job["fetch"] += 1

        fetched = []

        def split():
            i = at_job["split"]
            if i >= len(jobs):
                return
            _, a, n = jobs[i]
            before = used[i - PAIR] if i >= PAIR else None
            src = raw[:, i % RAW, 0:a * n]
            hi, lo = whi[:, i % PAIR, 0:a * n], wlo[:, i % PAIR, 0:a * n]
            split_hi.append(act.do(lambda: nc.scalar.copy(hi, src), fetched[i], before))
            split_lo.append(v_tt(lo, src, r32(hi), ALU.subtract, split_hi[i], before))
            at_job["split"] += 1
            fetch()

        def chunk():
            i = at_job["use"]
            while at_job["split"] <= min(i + PAIR - 1, len(jobs) - 1):
                split()
            at_job["use"] += 1
            _, a, n = jobs[i]
            hi = whi[:, i % PAIR, 0:a * n].rearrange("p (a n) -> p a n", a=a)
            lo = wlo[:, i % PAIR, 0:a * n].rearrange("p (a n) -> p a n", a=a)
            return hi, lo, split_lo[i]

        held_evac = []

        def settle():
            while held_evac:
                evac, i, bk, m = held_evac.pop(0)
                evac(i, bk, m)

        def gemm(steps, kt, cols, left, evac, carry=False, wait=True, by_half=False):
            taken, seen_k = {}, {}
            for i, k0, a in steps:
                hi, lo, m_w = chunk()
                if i not in taken:
                    taken[i] = (main.take(), main.take())
                    seen_k[i] = 0
                bk = taken[i]
                ends = seen_k[i] + a == kt
                halves = []
                for ts_ in ((0,), (1,)) if ends else ((0, 1),):
                    for kk in range(a):
                        lh, ll, m_l = left(k0 + kk)
                        mms = []
                        first, last = seen_k[i] + kk == 0, seen_k[i] + kk == kt - 1
                        for t in ts_:
                            o, ts = bk[t].ap[:, 0:cols], slice(t * P, (t + 1) * P)
                            mms += [(o, lh[:, ts], hi[:, kk, :], first, False),
                                    (o, lh[:, ts], lo[:, kk, :], False, False),
                                    (o, ll[:, ts], hi[:, kk, :], False, last)]
                        m = p_mm(mms, m_w, m_l, [bk[t].free for t in ts_] if first else None)
                    halves.append(m)
                seen_k[i] += a
                used.append(m)
                settle()
                if seen_k[i] == kt:
                    held_evac.append((evac, i, bk, halves if by_half else m))
                    if not wait:
                        settle()
                pump()
            if not carry:
                settle()
            return m

        ready = {}

        def done(key):
            if key not in ready:
                force(lambda: key in ready)
            return ready[key]

        def from_T(k):
            m = done(("T", k))
            return Th[:, k, :], Tl[:, k, :], m

        def to_parts(name, src, m_src, dst, ks, gain, free=None, after=None):
            ks = list(ks)
            groups = [ks[i:i + 2] for i in range(0, len(ks), 2)]
            n = 0
            held = []
            for g in groups:
                b = yield from takes(side)
                mt = p_tr([(b.ap[:, kk * S + t * P:kk * S + (t + 1) * P], src(n + kk, t))
                           for kk in range(len(g)) for t in range(2)], b.free, m_src)
                held.append((b, g, mt))
                n += len(g)
                if len(side.idle) == 0:
                    break
            trans = [h[2] for h in held]
            if after is not None:
                assert len(held) == len(groups)
                after(trans)
            yield
            while held:
                b, g, mt = held.pop(0)
                ah = []
                for kk, k in enumerate(g):
                    h, _ = dst(k)
                    sc = 1.0 if gain is None else gain[:, k:k + 1]
                    ah.append(a_copy(h, b.ap[:, kk * S:(kk + 1) * S], mt, trans, free, scale=sc))
                ms = []
                for kk, k in enumerate(g):
                    h, lo = dst(k)
                    if gain is None:
                        ms.append(v_tt(lo, b.ap[:, kk * S:(kk + 1) * S], r32(h), ALU.subtract, ah))
                    else:
                        ms.append(v_stt(lo, b.ap[:, kk * S:(kk + 1) * S], gain[:, k:k + 1], r32(h),
                                        ALU.mult, ALU.subtract, ah))
                    ready[(name, k)] = [ah[kk], ms[-1]]
                side.give(b, ms)
                if n < len(ks):
                    g = groups[n // 2]
                    b = yield from takes(side)
                    mt = p_tr([(b.ap[:, kk * S + t * P:kk * S + (t + 1) * P], src(n + kk, t))
                               for kk in range(len(g)) for t in range(2)], b.free, m_src)
                    held.append((b, g, mt))
                    trans.append(mt)
                    n += len(g)
                    yield

        st_at = [0]

        def stat(n):
            st_at[0] += n
            return ST[:, st_at[0] - n:st_at[0]]

        junk = [None]

        def square(src, acc, *after):
            junk[0] = a_fn(ACT.Square, JK[:, 0:src.shape[-1]], src, after, junk[0], acc=acc)
            return junk[0]

        def rstd_of(ss, n, width, out, *after):
            mean = stat(2)
            m = dve.do(lambda: nc.vector.reduce_sum(mean, ss.rearrange("p (t n) -> p t n", n=n), AX), after)
            m = v_ts(mean, mean, 1.0 / width, EPS, ALU.mult, ALU.add, m)
            return on_pool(lambda: nc.gpsimd.tensor_tensor(out, mean, mhalf, ALU.pow), m, m_half)

        m_ident = load(ident[:, :], A["c_main"][:, 0:128], "l_ident")
        mhalf = stat(2)
        m_half = on_pool(lambda: nc.gpsimd.memset(mhalf, -0.5))
        stage = lane("l_stage")
        m_stage = [load(STG[0:16, 0, :], A["attn_norm"].rearrange("l (k p) -> (l k) p", p=P), "l_g0")]
        m_freq = load(freq[:, :], A["c_main"][:, 512:560], "l_freq", q=pool, eng=nc.gpsimd)
        m_pos = load(PI[:, :], A["positions"].rearrange("b (t p) -> p (b t)", p=P), "l_pos", q=pool, eng=nc.gpsimd,
                     allow_slow_non_contiguous=True)
        r0 = 16
        for nm, rows in (("ffn_norm", 16), ("final_norm", 16), ("norm_g_2", 64), ("q_norm", 4), ("kv_norm", 2)):
            src = A[nm]
            src = {1: lambda s: s.rearrange("(k p) -> k p", p=P),
                   2: lambda s: s.rearrange("l (k p) -> (l k) p", p=P),
                   3: lambda s: s.rearrange("l g (k p) -> (l g k) p", p=P)}[len(src.shape)](src)
            m_stage.append(pool.dma(STG[r0:r0 + rows, 0, :], src, stage, eng=nc.gpsimd))
            r0 += rows
        for j in range(3):
            m_stage.append(pool.dma(STG[0:88, 1 + j, :], A["ffn_conv_2"][0, j].rearrange("(k p) -> k p", p=P),
                                   stage, eng=nc.gpsimd))
        x_v = A["x"].rearrange("b (t p) d -> p (b t) d", p=P)
        x_cut = [0, 256, 512, 1024, 1536, D]
        m_x = []
        for c, (lo, hi) in enumerate(zip(x_cut, x_cut[1:])):
            m_x.append(sp.dma(X[:, :, lo:hi], x_v[:, :, lo:hi], l_x[c], eng=nc.sync))
            for _ in range((1, 1, 2, 0, 0)[c]):
                fetch()
        m_mask = load(mask[:, :], A["c_main"][:, 128:512], "l_mask")
        tb = RA[0:32, 0, 0:32]
        oh = SG[0:32, 0, 0:384]
        ng = SG[0:32, 1, 0:384]
        m_tb = load(tb, A["rel_bias_table_2"], "l_tb")
        m_oh = load(oh, A["c_bias"][:, 0:384], "l_oh")
        m_ng = load(ng, A["c_bias"][:, 384:768], "l_ng")
        m_sk = load(SK[:, :], bass.AP(A["swa_sinks_2"].tensor, 0, [[0, P], [1, 32]]), "l_sk")

        def T_dst(k):
            return Th[:, k, :], Tl[:, k, :]

        def gains(b, rows, m):
            def go():
                return nc.tensor.transpose(b.ap[:, 0:rows], STG[0:rows, 0, :], ident[0:rows, 0:rows])
            return pe.do(go, m_ident, m, b.free)

        def keep_busy(n):
            b = side.take()
            side.give(b, p_mm([(b.ap[:, 0:P], ident[:, :], ident[:, :], True, True)] * n, m_ident, b.free))

        b = side.take()
        mt = gains(b, 16, m_stage[0])
        m_gt = a_copy(GT[:, 0:16], b.ap[:, 0:16], mt)
        side.give(b, m_gt)
        keep_busy(3)
        for c, (lo, hi) in enumerate(zip(x_cut, x_cut[1:])):
            spawn(to_parts("T", lambda i, t, lo=lo: X[:, t, lo + i * P:lo + (i + 1) * P], m_x[c],
                           T_dst, range(lo // P, hi // P), GT[:, 0:16], free=m_gt), (0, 0, 0, 2, 4)[c])
            if c < 2:
                pump()
                pump()
                split()
                keep_busy(5)
        m_gfn = []
        nat = Bufs([NAT[:, 0, :], NAT[:, 1, :]])

        def other_gains():
            b = yield from takes(side)
            mt = gains(b, 118, m_stage)

            def go():
                for j in range(1, 4):
                    last = nc.tensor.transpose(b.ap[:, j * P:j * P + 88], STG[0:88, j, :], ident[0:88, 0:88])
                return last
            mt = pe.do(go, mt)
            for z in nat.idle:
                z.free = [mt]
            yield
            m = a_copy(GT[:, 16:118], b.ap[:, 16:118], mt)
            m_cw = a_copy(CW[:, :, :], b.ap[:, P:512].rearrange("p (j k) -> p j k", j=3)[:, :, 0:88], mt)
            side.give(b, m_cw)
            m_gfn.append(v_tt(GFN[:, :], GT[:, 32:48], GT[:, 48:64], ALU.mult, m))
            ready["gains"] = m
        spawn(other_gains(), 4)
        rs_x = stat(2)

        def first_norm():
            ss = stat(10)
            m_ss = []
            for c, (lo, hi) in enumerate(zip(x_cut, x_cut[1:])):
                yield
                for t in range(2):
                    m_ss.append(square(X[:, t, lo:hi], ss[:, 5 * t + c:5 * t + c + 1], m_x[c]))
            ready["rs_x"] = rstd_of(ss, 5, D, rs_x, m_ss)
        spawn(first_norm(), 1)

        W96 = [RB[:, 0, 0:96], RB[:, 1, 0:96], RP[:, 0, 0:96], RP[:, 1, 0:96]]
        ang, nn, sn, cs = W96
        pf = stat(2)
        two_pi = 2 * math.pi

        def pieces(v, n):
            out = []
            for _ in range(n):
                e = math.floor(math.log2(abs(v)))
                q = 2.0 ** (e - 11)
                p = math.floor(v / q) * q
                out.append(p)
                v -= p
            return out

        m_trig = []

        def trig():
            m = dve.do(lambda: nc.vector.tensor_copy(pf, PI[:, :]), m_pos)
            for t in range(2):
                m2 = v_ts(ang[:, 48 * t:48 * t + 48], freq[:, :], pf[:, t:t + 1], None, ALU.mult, None, m, m_freq)
            m = m2
            for scale in (1024.0, 1.0):
                m = v_ts(nn, ang, 1.0 / (two_pi * scale), MAGIC, ALU.mult, ALU.add, m)
                m = v_ts(nn, nn, -MAGIC, None, ALU.add, None, m)
                yield
                for p in pieces(two_pi, 4):
                    m = v_stt(ang, nn, -p * scale, ang, ALU.mult, ALU.add, m)
                yield
            PIF = 3.1415925
            m_ang = v_ts(ang, ang, PIF, -PIF, ALU.min, ALU.max, m)
            m = v_ts(nn, ang, -1.0, None, ALU.mult, None, m_ang)
            m = v_tt(nn, nn, ang, ALU.max, m)
            m = v_ts(nn, nn, -1.0, math.pi / 2, ALU.mult, ALU.add, m)
            yield
            m_sin = a_fn(ACT.Sin, sn, ang, m_ang)
            m_cos = a_fn(ACT.Sin, cs, nn, m)
            yield
            c3, s3 = (z.rearrange("p (t f) -> p t f", t=2) for z in (cs, sn))
            for f0, d, o in ((0, 16, 0), (16, 32, 32)):
                if d == 32:
                    yield
                for h, sign in ((0, -1.0), (1, 1.0)):
                    oo = slice(o + h * d, o + h * d + d)
                    m_trig.append(v_ts(CS[:, :, oo], c3[:, :, f0:f0 + d], 1.0, None, ALU.mult, None, m_cos))
                    m_trig.append(v_ts(SN[:, :, oo], s3[:, :, f0:f0 + d], sign, None, ALU.mult, None, m_sin))
            ready["trig"] = m_trig
        spawn(trig(), 0)

        def bias_lines():
            b = yield from takes(side)
            mm = p_mm([(b.ap[0:32, 0:384], tb, oh, True, True)], m_tb, m_oh, b.free)
            yield
            ml = v_tt(oh, b.ap[0:32, 0:384], ng, ALU.add, mm, m_ng)
            side.give(b, ml)
            ready["lines"] = load(lines[:, :], oh, "l_lines", ml, q=pool, eng=nc.gpsimd)

        spawn(bias_lines())

        rope_last = []

        def rope(nat, off, d, c0, out, *after):
            nh = nat.shape[2]
            if not rope_last:
                rope_last.append(ready["trig"])
            ra = RA[:, :, 0:nh * 2 * d].rearrange("p t (h e) -> p t h e", h=nh)
            rb = RB[:, :, 0:nh * 2 * d].rearrange("p t (h e) -> p t h e", h=nh)

            def tab(z, lo, n):
                return z[:, :, lo:lo + n].unsqueeze(2).to_broadcast([P, 2, nh, n])
            m1 = v_tt(ra, nat[:, :, :, off:off + 2 * d], tab(CS, c0, 2 * d), ALU.mult, after, rope_last)
            m2 = v_tt(rb[:, :, :, 0:d], nat[:, :, :, off + d:off + 2 * d], tab(SN, c0, d), ALU.mult, after, rope_last)
            m3 = v_tt(rb[:, :, :, d:2 * d], nat[:, :, :, off:off + d], tab(SN, c0 + d, d), ALU.mult, after, rope_last)
            m4 = v_tt(out, ra, rb, ALU.add, m1, m2, m3)
            rope_last[0] = m4
            return m4

        def take_now(bufs):
            if not bufs.idle:
                force(lambda: bufs.idle)
            return bufs.take()

        ss_q, ss_kv = stat(2), stat(2)
        rs_q, rs_kv = stat(2), stat(2)
        rp_free = [None]

        def C_dst(k):
            return CTh[:, k, :], CTl[:, k, :]

        def evac_c(i, bk, m):
            n = (512, 320)[i]
            done("rs_x")
            done("gains")
            nb = take_now(nat)
            nv = nb.ap.rearrange("p (t n) -> p t n", t=2)[:, :, 0:n]
            me = [a_copy(nv[:, t, :], bk[t].ap[:, 0:n], m, ready["rs_x"], nb.free, scale=rs_x[:, t:t + 1]) for t in range(2)]
            for t in range(2):
                main.give(bk[t], me[t])
            if i == 0:
                mq = [square(nv[:, t, :], ss_q[:, t:t + 1], me[t]) for t in range(2)]
                ready["rs_q"] = rstd_of(ss_q, 1, 512, rs_q, mq)
                spawn(to_parts("C", lambda k, t: nv[:, t, k * P:(k + 1) * P], me, C_dst, range(4),
                               GT[:, 112:118], after=lambda tr: nat.give(nb, tr, mq)))
                return
            mq = [square(nv[:, t, 0:256], ss_kv[:, t:t + 1], me[t]) for t in range(2)]
            ready["rs_kv"] = rstd_of(ss_kv, 1, 256, rs_kv, mq)

            def key_rope():
                while "trig" not in ready:
                    yield
                z = on_pool(lambda: nc.gpsimd.memset(KR[64:128, 0, :], 0.0))
                z2 = on_pool(lambda: nc.gpsimd.memset(KR[0:64, 1, :], 0.0))
                rp = RP[:, :, :].rearrange("p t (h e) -> p t h e", h=2)
                kin = nv[:, :, 256:320].unsqueeze(2)
                mr = rope(kin, 0, 32, 32, rp[:, :, 0:1, :], me, rp_free[0])
                mr2 = v_ts(rp[:, :, 1, :], rp[:, :, 0, :], 1.0, None, ALU.mult, None, mr)
                yield
                bb = yield from takes(side)
                mt = p_tr([(bb.ap[:, t * P:(t + 1) * P], RP[:, t, :]) for t in range(2)], mr2, bb.free)
                rp_free[0] = mt
                yield
                m1 = a_copy(KR[0:64, 0, :], bb.ap[0:64, 0:S], mt)
                m2 = a_copy(KR[64:128, 1, :], bb.ap[64:128, 0:S], mt)
                side.give(bb, m1, m2)
                ready["kr"] = [m1, m2, z, z2]
                kr_rope.append(mr)
                yield
            kr_rope = []
            gk = key_rope()
            spawn(gk)
            spawn(to_parts("C", lambda k, t: nv[:, t, k * P:(k + 1) * P], me, C_dst, range(4, 6),
                           GT[:, 112:118], after=lambda tr: ready.__setitem__("ckv_tr", tr)))

            def release():
                while "kr" not in ready or "ckv_tr" not in ready:
                    yield
                nat.give(nb, ready["ckv_tr"], mq, kr_rope)
            spawn(release())

        gemm_c = jc[0]
        cs0 = [s for s in gemm_c if s[0] == 0]
        cs1 = [s for s in gemm_c if s[0] == 1]
        gemm(cs0, KT, 512, from_T, evac_c)
        gemm(cs1, KT, 320, from_T, evac_c)

        def heads_to_T(name, nb, nv, me, dst, h0, nh, off, width, rope_args=None, extra=None):
            mr = me
            if rope_args:
                mr = [rope(nv, *rope_args, nv[:, :, :, rope_args[0]:rope_args[0] + 2 * rope_args[1]], me), me]
                yield
            trs, outs = [], []
            for h in range(0, nh, 2):
                bb = yield from takes(side)
                mt = p_tr([(bb.ap[:, hh * S + t * P:hh * S + (t + 1) * P], nv[:, t, h + hh, off:off + P])
                           for hh in range(2) for t in range(2)], mr, bb.free)
                trs.append(mt)
                outs.append((h, bb, mt))
            if nb is not None:
                nat.give(nb, trs)
            yield
            for h, bb, mt in outs:
                mo = a_copy(dst[:, h0 + h:h0 + h + 2, :], bb.ap.rearrange("p (h s) -> p h s", h=2), mt)
                side.give(bb, mo)
                for hh in range(2):
                    ready[(name, h0 + h + hh)] = mo

        def evac_qkv(i, bk, m):
            if i < 4:
                nb = take_now(nat)
                nv = nb.ap.rearrange("p (t n) -> p t n", t=2)
                me = [a_copy(nv[:, t, :], bk[t].ap, m, ready["rs_x"], nb.free, scale=rs_x[:, t:t + 1]) for t in range(2)]
                dst, nm = ((QT, "q"), (KTt, "k"))[i // 2]
                spawn(heads_to_T(nm, nb, nv.rearrange("p t (h e) -> p t h e", h=4), me, dst, 4 * (i % 2), 4, 0, P,
                                 (0, 16, 0)))
            else:
                me = [a_copy(V[:, t, 512 * (i - 4):512 * (i - 3)], bk[t].ap, m, ready["rs_x"], scale=rs_x[:, t:t + 1])
                      for t in range(2)]
                for h in range(4):
                    ready[("v", 4 * (i - 4) + h)] = me
            for t in range(2):
                main.give(bk[t], me[t])

        gemm(jqkv, KT, 512, from_T, evac_qkv)

        sbufs = Bufs([S1[:, i, :] for i in range(4)])
        ptbufs = Bufs([PT1[:, i, :] for i in range(2)])
        stats = Bufs([AS[:, i, :] for i in range(6)])
        alive = [0]
        for z in sbufs.idle:
            z.free = [done("lines")]

        def head(tag, h, scale, rope_part, y):
            alive[0] += 1
            m_q, m_k, m_v = ([done_now(x) for x in ((tag + "q", h), (tag + "k", h), (tag + "v", h))])
            deps = [m_q, m_k]
            if rope_part:
                deps += [done_now(("mqr", h)), ready["kr"]]
            bb = yield from takes(side)
            mms = []
            for t, (o, n) in enumerate(((0, P), (P, S))):
                ts = slice(t * P, (t + 1) * P)
                out = bb.ap[:, o:o + n]
                mms.append((out, QT[:, h, ts], KTt[:, h, 0:n], True, not rope_part))
                if rope_part:
                    mms.append((out, QR[:, h // 2, ts], KR[:, h % 2, 0:n], False, True))
            m1 = p_mm(mms, deps, bb.free)
            yield
            sbuf = yield from takes(sbufs)
            st = yield from takes(stats)
            s, a = sbuf.ap, st.ap
            m2 = v_stt(s, bb.ap[:, 0:384], scale, mask[:, :], ALU.mult, ALU.add, m1, m_mask, sbuf.free)
            side.give(bb, m2)
            m3 = v_max(a[:, 0:1], s[:, 0:P], m2, st.free)
            m4 = v_max(a[:, 1:2], s[:, P:384], m2, st.free)
            m5 = v_ts(a[:, 2:4], a[:, 0:2], -1.0, None, ALU.mult, None, m3, m4)
            yield
            m6 = [a_fn(ACT.Exp, s[:, lo:hi], s[:, lo:hi], m5, bias=a[:, 2 + t:3 + t], acc=a[:, 4 + t:5 + t])
                  for t, (lo, hi) in enumerate(((0, P), (P, 384)))]
            yield
            m7 = dve.do(lambda: nc.vector.reciprocal(a[:, 6:8], a[:, 4:6]), m6)
            m8 = [v_ts(s[:, lo:hi], s[:, lo:hi], a[:, 6 + t:7 + t], None, ALU.mult, None, m7)
                  for t, (lo, hi) in enumerate(((0, P), (P, 384)))]
            stats.give(st, m8)
            yield
            bb = yield from takes(side)
            m9 = p_tr([(bb.ap[:, i * P:(i + 1) * P], s[:, i * P:(i + 1) * P]) for i in range(3)], m8, bb.free)
            sbufs.give(sbuf, m9)
            yield
            pt = yield from takes(ptbufs)
            m10 = a_copy(pt.ap, bb.ap[:, 0:384], m9, pt.free)
            side.give(bb, m10)
            yield
            bb = yield from takes(side)
            hs = slice(h * P, (h + 1) * P)
            m11 = p_mm([(bb.ap[:, 0:S], V[:, 0, hs], pt.ap[:, 0:S], True, False),
                        (bb.ap[:, P:S], V[:, 1, hs], pt.ap[:, S:384], False, True)], m10, m_v, bb.free)
            ptbufs.give(pt, m11)
            yield
            m12 = a_copy(YF[:, y + h, :], bb.ap[:, 0:S], m11)
            side.give(bb, m12)
            ready[("y", y + h)] = m12
            alive[0] -= 1

        def done_now(key):
            return ready[key]

        def heads(tag, scale, rope_part, y, at_once):
            for h in range(8):
                keys = [(tag + "q", h), (tag + "k", h), (tag + "v", h)] + ([("mqr", h), "kr"] if rope_part else [])
                while alive[0] >= at_once or any(k not in ready for k in keys):
                    yield
                spawn(head(tag, h, scale, rope_part, y))
                yield

        spawn(heads("", P ** -0.5, False, 0, 3))

        def evac_gate(i, bk, m, base=0):
            n, ab = divmod(base + i, 2)
            me = [a_copy(G[:, n, ab, 0, :], bk[0].ap, m, ready["rs_x"], scale=rs_x[:, 0:1]),
                  v_ts(G[:, n, ab, 1, :], bk[1].ap, rs_x[:, 1:2], None, ALU.mult, None, m, ready["rs_x"])]
            for t in range(2):
                main.give(bk[t], me[t])
            ready[("g", n, ab)] = me

        gemm(jg1, KT, 512, from_T, evac_gate)
        force(lambda: all(("y", h) in ready for h in range(8)))

        def from_C(k0):
            def left(k):
                m = done(("C", k0 + k))
                return CTh[:, k0 + k, :], CTl[:, k0 + k, :], m
            return left

        done("rs_q")
        done("kr")

        def evac_uq(i, bk, m):
            nb = take_now(nat)
            nv = nb.ap.rearrange("p (t n) -> p t n", t=2)[:, :, 0:384]
            me = [a_copy(nv[:, 0, :], bk[0].ap[:, 0:384], m, ready["rs_q"], nb.free, scale=rs_q[:, 0:1]),
                  v_ts(nv[:, 1, :], bk[1].ap[:, 0:384], rs_q[:, 1:2], None, ALU.mult, None, m, ready["rs_q"], nb.free)]
            for t in range(2):
                main.give(bk[t], me[t])
            n4_ = nv.rearrange("p t (h e) -> p t h e", h=2)

            def go():
                mr = rope(n4_, P, 32, 32, RP[:, :, :].rearrange("p t (h e) -> p t h e", h=2), me, rp_free[0])
                yield
                bb = yield from takes(side)
                mt = p_tr([(bb.ap[:, hh * S + t * P:hh * S + (t + 1) * P], n4_[:, t, hh, 0:P])
                           for hh in range(2) for t in range(2)], me, bb.free)
                b2 = yield from takes(side)
                mt2 = p_tr([(b2.ap[:, t * P:(t + 1) * P], RP[:, t, :]) for t in range(2)], mr, b2.free)
                rp_free[0] = mt2
                nat.give(nb, mt, mr)
                yield
                mo = a_copy(QT[:, 2 * i:2 * i + 2, :], bb.ap.rearrange("p (h s) -> p h s", h=2), mt)
                side.give(bb, mo)
                m2 = a_copy(QR[:, i, :], b2.ap[:, 0:S], mt2)
                side.give(b2, m2)
                for hh in range(2):
                    ready[("mq", 2 * i + hh)] = mo
                    ready[("mqr", 2 * i + hh)] = m2
            spawn(go())

        gemm(juq, 4, 384, from_C(0), evac_uq)
        done("rs_kv")

        def evac_ukv(i, bk, m):
            nb = take_now(nat)
            nv = nb.ap.rearrange("p (t n) -> p t n", t=2)[:, :, 0:S]
            me, mv = [], []
            for t in range(2):
                src = bk[t].ap.rearrange("p (h n) -> p h n", h=2)
                ko = nv[:, t, :].rearrange("p (h e) -> p h e", h=2)
                vo = V[:, t, 2 * i * P:(2 * i + 2) * P].rearrange("p (h e) -> p h e", h=2)
                if t == 0:
                    me.append(a_copy(ko, src[:, :, 0:P], m, ready["rs_kv"], nb.free, scale=rs_kv[:, t:t + 1]))
                    mv.append(a_copy(vo, src[:, :, P:S], m, scale=rs_kv[:, t:t + 1]))
                else:
                    me.append(v_ts(ko, src[:, :, 0:P], rs_kv[:, t:t + 1], None, ALU.mult, None, m, ready["rs_kv"], nb.free))
                    mv.append(v_ts(vo, src[:, :, P:S], rs_kv[:, t:t + 1], None, ALU.mult, None, m))
                main.give(bk[t], me[t], mv[t])
            for hh in range(2):
                ready[("mv", 2 * i + hh)] = mv
            spawn(heads_to_T("mk", nb, nv.rearrange("p t (h e) -> p t h e", h=2), me, KTt, 2 * i, 2, 0, P))

        gemm(jukv, 2, 512, from_C(4), evac_ukv, wait=False)
        spawn(heads("m", (P + 64) ** -0.5, True, 8, 3))

        def y_parts(h):
            return (CTh[:, h, :], CTl[:, h, :]) if h < 6 else (Th[:, h, :], Tl[:, h, :])

        def split_y(hs, m_free):
            for h in hs:
                while ("y", h) not in ready:
                    yield
                hi, lo = y_parts(h)
                mh = a_copy(hi, YF[:, h, :], ready[("y", h)], m_free)
                ml = v_tt(lo, YF[:, h, :], r32(hi), ALU.subtract, mh, m_free)
                ready[("Y", h)] = [mh, ml]
                if h % 2:
                    yield
        spawn(split_y(range(6), used[-1]), 4)
        m_xT = gemm(jg2, KT, 512, from_T, lambda i, bk, m: evac_gate(i, bk, m, 4))
        spawn(split_y(range(6, 16), m_xT))

        def from_Y(h0):
            def left(k):
                m = done(("Y", h0 + k))
                return (*y_parts(h0 + k), m)
            return left

        part = {}

        def branch_evac(n, ab):
            def evac(i, bk, m):
                g = G[:, n, ab, :, :]
                mg = a_fn(ACT.Sigmoid, g, g, ready[("g", n, ab)])
                me = [v_tt(g[:, t, :], bk[t].ap, g[:, t, :], ALU.mult, m, mg) for t in range(2)]
                for t in range(2):
                    main.give(bk[t], me[t])
                if ab == 0:
                    part[n] = me
                    return
                ga = G[:, n, 0, :, :]
                mm = v_tt(ga, ga, g, ALU.add, me, part[n])

                def dst(k):
                    return MT[:, n, 0, k, :], MT[:, n, 1, k, :]
                spawn(to_parts(("M", n), lambda k, t: G[:, n, 0, t, k * P:(k + 1) * P], mm, dst, range(4), None))
            return evac

        for n in range(4):
            gemm(jbr[n][0], 8, 512, from_Y(0), branch_evac(n, 0))
            gemm(jbr[n][1], 8, 512, from_Y(8), branch_evac(n, 1))
        m_yT = used[-1]

        def from_M(k):
            n, kk = divmod(k, 4)
            m = done((("M", n), kk))
            return MT[:, n, 0, kk, :], MT[:, n, 1, kk, :], m

        def residual(name_gain, ss_, out_marks, m_free):
            def evac(i, bk, m):
                cs_ = slice(512 * i, 512 * (i + 1))
                me = [v_tt(X[:, t, cs_], bk[t].ap, X[:, t, cs_], ALU.add, m) for t in range(2)]
                for t in range(2):
                    main.give(bk[t], me[t])
                    out_marks.append(square(X[:, t, cs_], ss_[:, 4 * t + i:4 * t + i + 1], me[t]))
                for k in range(4 * i, 4 * i + 4):
                    ready.pop(("T", k), None)
                spawn(to_parts("T", lambda k, t: X[:, t, (4 * i + k) * P:(4 * i + k + 1) * P], me,
                               T_dst, range(4 * i, 4 * i + 4), name_gain, free=m_free,
                               after=lambda tr: x_read.extend(tr)))
            return evac

        x_read = []
        ss2 = stat(8)
        rs2 = stat(2)
        m_ss2 = []
        for k in range(KT):
            ready.pop(("T", k), None)
        gemm(jout, KT, 512, from_M, residual(GT[:, 16:32], ss2, m_ss2, m_yT))
        m_rs2 = rstd_of(ss2, 4, D, rs2, m_ss2)

        sg_buf = Bufs([SG[:, :, :]])
        hid_buf = Bufs([HID[:, i, :, :] for i in range(2)])
        sg_now = {}

        def evac_gate1(i, bk, m):
            z = take_now(sg_buf)
            me = [a_fn(ACT.Silu, z.ap[:, t, :], bk[t].ap, m, m_rs2, z.free, scale=rs2[:, t:t + 1]) for t in range(2)]
            for t in range(2):
                main.give(bk[t], me[t])
            sg_now[0] = (z, me)

        def H_dst(k):
            return Hh[:, k, :], Hl[:, k, :]

        def evac_up1(f):
            def evac(i, bk, m):
                z, mg = sg_now[0]
                hb = take_now(hid_buf)
                me = [v_stt(hb.ap[:, t, :], bk[t].ap, rs2[:, t:t + 1], z.ap[:, t, :], ALU.mult, ALU.mult,
                            m, mg, hb.free) for t in range(2)]
                for t in range(2):
                    main.give(bk[t], me[t])
                sg_buf.give(z, me)
                spawn(to_parts("H", lambda k, t: hb.ap[:, t, k * P:(k + 1) * P], me, H_dst,
                               range(4 * f, 4 * f + 4), None, after=lambda tr: hid_buf.give(hb, tr)))
            return evac

        for f in range(NF):
            gemm(jff[f][0], KT, 512, from_T, evac_gate1)
            gemm(jff[f][1], KT, 512, from_T, evac_up1(f))
        m_ff = used[-1]

        def from_H(k):
            m = done(("H", k))
            return Hh[:, k, :], Hl[:, k, :], m

        ss3, rs3 = stat(8), stat(2)
        m_ss3 = []
        x_read.clear()
        gb_v = bass.AP(A["final_norm"].tensor, 0, [[0, P], [1, D]])
        m_gf = load(GB[:, :], gb_v, "l_gf", [z.free for z in nat.idle], q=pool, eng=nc.gpsimd)
        m_down = gemm(jdown, FT, 512, from_H, residual(GFN[:, :], ss3, m_ss3, [m_ff, m_gfn]))
        m_rs3 = rstd_of(ss3, 4, D, rs3, m_ss3)

        ss4, rs4, rs34 = stat(8), stat(2), stat(2)

        def norm_between():
            while any(("T", k) not in ready for k in range(KT)):
                yield
            marks = []
            for c in range(4):
                for t in range(2):
                    xs = X[:, t, 512 * c:512 * (c + 1)]
                    mx = v_stt(xs, xs, rs3[:, t:t + 1], GB[:, 512 * c:512 * (c + 1)], ALU.mult, ALU.mult,
                               m_rs3, m_gf, x_read)
                    ready[("xb", c, t)] = mx
                yield
                for t in range(2):
                    xs = X[:, t, 512 * c:512 * (c + 1)]
                    marks.append(square(xs, ss4[:, 4 * t + c:4 * t + c + 1], ready[("xb", c, t)]))
            mr = rstd_of(ss4, 4, D, rs4, marks)
            ready["rs34"] = v_tt(rs34, rs3, rs4, ALU.mult, mr, m_rs3)
            ready["gb"] = [ready[("xb", c, t)] for c in range(4) for t in range(2)]
        spawn(norm_between())

        m_kz = [on_pool(lambda: nc.gpsimd.memset(KK[64:128, :, 0, :], 0.0), m_down),
                on_pool(lambda: nc.gpsimd.memset(KK[0:64, :, 1, :], 0.0), m_down)]
        l_bt = [lane("l_bt0"), lane("l_bt1")]
        bt = {}

        def load_bias(c, *after):
            src = bass.AP(lines, 8 * c * 384, [[1, P], [384, 8], [1, S]])
            bt[c] = pool.dma(BT[:, c % 2, :, :], src, l_bt[c % 2], after, eng=nc.gpsimd)

        for c in range(2):
            load_bias(c, m_down, done("lines"))

        def bt_view(c, e, n):
            base = BT[:, c % 2, 2 * e:2 * e + 2, 0:n]
            pat = [list(z) for z in base.ap]
            pat[-1] = [-1, n]
            return bass.AP(base.tensor, base.offset + n - 1, pat)

        pairs = {"n": 0, "bt": {0: [], 1: [], 2: [], 3: []}}
        sb2 = Bufs([S2a[:, 0, :], S2a[:, 1, :], S2b[:, 0, :], S2b[:, 1, :]])
        pt2 = Bufs([PT2[:, 0, :], PT2[:, 1, :]])
        for z in sb2.idle + pt2.idle:
            z.free = [m_down]
        qp = Bufs([QP[:, 0, :, :], QP[:, 1, :, :]])

        def pair(c, e, qb):
            j = 4 * c + e
            g = j // 2
            st = yield from takes(stats)
            a = st.ap
            b0 = yield from takes(side)
            b1 = yield from takes(side)
            m1 = p_mm([(b0.ap[:, 0:S], qb.ap[:, e, 0:P], KK[:, g, :, 0:P], True, True)],
                      ready[("q2", c)], ready[("k2", g)], b0.free)
            m1b = p_mm([(b1.ap, qb.ap[:, e, P:S], KK[:, g, :, :].rearrange("p a s -> p (a s)"), True, True)], b1.free)
            pairs[("qp", c)].append(m1b)
            if len(pairs[("qp", c)]) == 4:
                qp.give(qb, pairs[("qp", c)])
            yield
            sbuf = yield from takes(sb2)
            s = sbuf.ap
            m2 = v_stt(s[:, 0:S].rearrange("p (h n) -> p h n", h=2), b0.ap[:, 0:S].rearrange("p (h n) -> p h n", h=2),
                       0.125, bt_view(c, e, P), ALU.mult, ALU.add, m1, bt[c], sbuf.free)
            side.give(b0, m2)
            m3 = v_stt(s[:, S:768].rearrange("p (h n) -> p h n", h=2), b1.ap.rearrange("p (h n) -> p h n", h=2),
                       0.125, bt_view(c, e, S), ALU.mult, ALU.add, m1b, bt[c], sbuf.free)
            side.give(b1, m3)
            pairs["bt"][c] += [m2, m3]
            if len(pairs["bt"][c]) == 8 and c < 2:
                load_bias(c + 2, pairs["bt"][c])
            m4 = v_max(a[:, 0:2], s[:, 0:S].rearrange("p (h n) -> p h n", h=2), m2, st.free)
            m5 = v_max(a[:, 2:4], s[:, S:768].rearrange("p (h n) -> p h n", h=2), m3, st.free)
            av = a[:, 0:4].rearrange("p (t h) -> p t h", t=2)
            dv = a[:, 4:8].rearrange("p (t h) -> p t h", t=2)
            sk = SK[:, 2 * j:2 * j + 2].unsqueeze(1).to_broadcast([P, 2, 2])
            m6 = v_tt(av, av, sk, ALU.max, m4, m5, m_sk)
            m7 = v_tt(dv, sk, av, ALU.subtract, m6)
            m8 = v_ts(a[:, 12:16], a[:, 0:4], -1.0, None, ALU.mult, None, m6)
            yield
            parts = ((0, 128), (128, 256), (256, 512), (512, 768))
            m9 = [a_fn(ACT.Exp, s[:, lo:hi], s[:, lo:hi], m8, bias=a[:, 12 + i:13 + i], acc=a[:, 8 + i:9 + i])
                  for i, (lo, hi) in enumerate(parts)]
            m9.append(a_fn(ACT.Exp, a[:, 4:8], a[:, 4:8], m7))
            yield
            m10 = v_tt(a[:, 8:12], a[:, 8:12], a[:, 4:8], ALU.add, m9)
            m11 = dve.do(lambda: nc.vector.reciprocal(a[:, 12:16], a[:, 8:12]), m10)
            m12 = [v_ts(s[:, lo:hi], s[:, lo:hi], a[:, 12 + i:13 + i], None, ALU.mult, None, m11)
                   for i, (lo, hi) in enumerate(parts[:2])]
            yield
            m12 += [a_copy(s[:, lo:hi], s[:, lo:hi], m11, scale=a[:, 14 + i:15 + i])
                   for i, (lo, hi) in enumerate(parts[2:])]
            stats.give(st, m12)
            yield
            c0 = yield from takes(side)
            c1 = yield from takes(side)
            m13 = p_tr([(c0.ap[:, i * P:(i + 1) * P], s[:, o:o + P]) for i, o in enumerate((0, 256, 128, 512))],
                       m12, c0.free)
            m14 = p_tr([(c1.ap[:, i * P:(i + 1) * P], s[:, o:o + P]) for i, o in enumerate((384, 640))], c1.free)
            sb2.give(sbuf, m14)
            yield
            pt = yield from takes(pt2)
            m15 = a_copy(pt.ap[:, 0:512], c0.ap, m13, pt.free)
            m16 = v_ts(pt.ap[:, 512:768], c1.ap[:, 0:S], 1.0, None, ALU.mult, None, m14, pt.free)
            side.give(c0, m15)
            side.give(c1, m16)
            while "v2" not in ready:
                yield
            yield
            o = yield from takes(side)
            kts = o.ap.rearrange("p (h n) -> p h n", h=2)[:, :, P:S]
            m17 = p_mm([(o.ap, VV[:, 0, g, :, :].rearrange("p a e -> p (a e)"), pt.ap[:, 0:512], True, False),
                        (kts, VV[:, 1, g, :, :].rearrange("p a e -> p (a e)"), pt.ap[:, 512:768].rearrange(
                            "p (h n) -> p h n", h=2), False, True)], m15, m16, ready["v2"], o.free)
            pt2.give(pt, m17)
            yield
            mh = [a_copy(YH[64 * z:64 * z + 64, j, :], o.ap[64 * z:64 * z + 64, S * z:S * z + S], m17)
                  for z in range(2)]
            ml = [v_tt(YL[64 * z:64 * z + 64, j, :], o.ap[64 * z:64 * z + 64, S * z:S * z + S],
                       r32(YH[64 * z:64 * z + 64, j, :]), ALU.subtract, mh) for z in range(2)]
            side.give(o, ml)
            ready[("Y2", j)] = [mh, ml]
            pairs["n"] -= 1

        def evac_in2(i, bk, m):
            if i == 0:
                rs = done("rs34")
                nbs = []
                nats = [take_now(nat), take_now(nat)]
                for t in range(2):
                    nv = nats[t].ap.rearrange("p (g a e) -> p g a e", g=8, a=2)
                    src = bk[t].ap.rearrange("p (g e) -> p g e", g=8)
                    ma = a_copy(nv[:, :, 0, :], src, m, rs, nats[t].free, ready["gb"], scale=rs34[:, t:t + 1])
                    mb = v_ts(nv[:, :, 1, :], src, rs34[:, t:t + 1], None, ALU.mult, None, ma, nats[t].free, ready["gb"])
                    main.give(bk[t], ma, mb)
                    nbs.append((nv, [ma, mb]))

                def go():
                    trs = []
                    for g in range(0, 8, 2):
                        bb = yield from takes(side)
                        mt = p_tr([(bb.ap[:, gg * S + t * P:gg * S + (t + 1) * P],
                                    nbs[t][0][:, g + gg, :, :].rearrange("p a e -> p (a e)"))
                                   for gg in range(2) for t in range(2)], nbs[0][1], nbs[1][1], bb.free)
                        trs.append(mt)
                        yield
                        bv = bb.ap.rearrange("p (g s) -> p g s", g=2)
                        mo = [a_copy(KK[64 * z:64 * z + 64, g:g + 2, z, :], bv[64 * z:64 * z + 64], mt, m_kz)
                              for z in range(2)]
                        side.give(bb, mo)
                        ready[("k2", g)] = ready[("k2", g + 1)] = [mo, m_kz]
                    for z in nats:
                        nat.give(z, trs)
                spawn(go())
                return
            if i == 2:
                mv = []
                for t in range(2):
                    src = bk[t].ap.rearrange("p (g e) -> p g e", g=8)
                    ma = a_copy(VV[:, t, :, 0, :], src, m, scale=rs34[:, t:t + 1])
                    mb = v_ts(VV[:, t, :, 1, :], src, rs34[:, t:t + 1], None, ALU.mult, None, ma)
                    main.give(bk[t], ma, mb)
                    mv += [ma, mb]
                ready["v2"] = mv
                return
            c = max(i - 2, 0)
            nb = take_now(nat)
            nv = nb.ap.rearrange("p (t n) -> p t n", t=2)
            me = [a_copy(nv[:, t, :], bk[t].ap, m, nb.free, scale=rs34[:, t:t + 1]) for t in range(2)]
            for t in range(2):
                main.give(bk[t], me[t])
            pairs[("qp", c)] = []

            def go():
                qb = yield from takes(qp)
                held, trs = [], []
                for e in range(0, 4, 2):
                    bb = yield from takes(side)
                    mt = p_tr([(bb.ap[:, ee * S + t * P:ee * S + (t + 1) * P], nv[:, t, (e + ee) * P:(e + ee + 1) * P])
                               for ee in range(2) for t in range(2)], me, bb.free)
                    held.append((e, bb, mt))
                    trs.append(mt)
                nat.give(nb, trs)
                nat_last[c] = trs
                yield
                mo = []
                for e, bb, mt in held:
                    mo.append(a_copy(qb.ap[:, e:e + 2, :], bb.ap.rearrange("p (h s) -> p h s", h=2), mt, qb.free))
                    side.give(bb, mo[-1])
                ready[("q2", c)] = mo
                yield
                for e in range(4):
                    while pairs["n"] >= 4:
                        yield
                    pairs["n"] += 1
                    spawn(pair(c, e, qb))
                    yield
            spawn(go())

        nat_last = {}
        gemm(jin2, KT, 512, from_T, evac_in2, True)
        m_T2 = used[-1]

        def gain_1():
            while 3 not in nat_last:
                yield
            ready["g1"] = load(GB[:, :], bass.AP(A["norm_g_2"].tensor, D, [[0, P], [1, D]]), "l_g1",
                               list(nat_last.values()), q=pool, eng=nc.gpsimd)
        spawn(gain_1())

        def from_Y2(k):
            m = done(("Y2", k))
            return YH[:, k, :], YL[:, k, :], m

        def evac_post(dst, gb, k_gb, ss_, marks, m_free):
            def evac(i, bk, m):
                cs_ = slice(512 * i, 512 * (i + 1))
                mqs = [square(bk[t].ap, ss_[:, 4 * t + i:4 * t + i + 1], m[t]) for t in range(2)]
                if i == 3:
                    marks[3] = (bk, mqs)
                    return
                for t, mq in enumerate(mqs):
                    mg = v_tt(dst[:, t, cs_], bk[t].ap, gb[:, cs_], ALU.mult, mq, done(k_gb), m_free)
                    main.give(bk[t], mg)
                    marks[(i, t)] = (mq, mg)
            return evac

        ss5, rs5, ss6, rs6 = stat(8), stat(2), stat(8), stat(2)
        mk5 = {}
        m_part = {}

        def evac_part(i, bk, m):
            m_part[i] = [a_copy(PR[:, i - 2, t, :], bk[t].ap, m) for t in range(2)]
            for t in range(2):
                main.give(bk[t], m_part[i][t])

        def evac_rest(i, bk, m):
            ma = []
            for t in range(2):
                o = PR[:, i - 2, t, :]
                ma.append(v_tt(o, bk[t].ap, o, ALU.add, m[t], m_part[i]))
                main.give(bk[t], ma[t])
            m_sq5[i] = [square(PR[:, i - 2, t, :], ss5[:, 4 * t + i:4 * t + i + 1], ma[t]) for t in range(2)]
            if i == 2:
                gain_rest(i)

        def gain_rest(i):
            cs_ = slice(512 * i, 512 * (i + 1))
            for t in range(2):
                mk5[(i, t)] = (m_sq5[i], v_tt(MG[:, t, cs_], PR[:, i - 2, t, :], GB[:, cs_], ALU.mult,
                                              done("g1"), m_sq5[i]))

        m_sq5 = {}
        gemm(jout2[0], half, 512, from_Y2, evac_part)
        gemm(jout2[1], KT, 512, from_Y2, evac_post(MG, GB, "g1", ss5, mk5, None), wait=False, by_half=True)
        gemm(jout2[2], half, 512, from_Y2, evac_rest, by_half=True)
        m_out2 = used[-1]
        m_rs5 = rstd_of(ss5, 4, D, rs5, [v[0] for v in mk5.values()], m_sq5[3])
        for k in range(KT):
            ready.pop(("T", k), None)
        x_read.clear()
        m_xc = {}

        def update(c):
            free = [m_T2, [mk5[(c, t)] for t in range(2)] if c > 1 else None]
            m_xc[c] = [[], []]
            step = 256 if c == 0 else 512
            for lo in range(512 * c, 512 * (c + 1), step):
                xs = slice(lo, lo + step)
                me = [v_stt(X[:, t, xs], MG[:, t, xs], rs5[:, t:t + 1], X[:, t, xs], ALU.mult, ALU.add,
                            m_rs5, mk5[(c, t)][1], ready[("xb", c, t)]) for t in range(2)]
                for t in range(2):
                    m_xc[c][t].append(me[t])
                spawn(to_parts("T", lambda k, t, lo=lo: X[:, t, lo + k * P:lo + (k + 1) * P], me,
                               T_dst, range(lo // P, (lo + step) // P), GT[:, 80:96], free=free), 0)

        def squares(c):
            return [square(X[:, t, 512 * c:512 * (c + 1)], ss6[:, 4 * t + c:4 * t + c + 1], m_xc[c][t])
                    for t in range(2)]

        def update_2():
            update(2)
            spawn(update_3(), 2)
            yield
            ready["sq6"] += squares(1)
            gain_rest(3)
            yield
            ready["sq6"] += squares(2)

        def update_3():
            ready["g3"] = load(GB[:, :], bass.AP(A["norm_g_2"].tensor, 3 * D, [[0, P], [1, D]]), "l_g3",
                               [v[1] for v in mk5.values()], q=pool, eng=nc.gpsimd)
            update(3)
            yield
            ready["rs6"] = rstd_of(ss6, 4, D, rs6, ready["sq6"], squares(3))
            spawn(row_factor(), 0)

        keep_busy(18)
        update(0)
        pump()
        pump()
        update(1)
        ready["sq6"] = squares(0)
        spawn(update_2(), 0)

        R = RP[:, :, :].rearrange("p t s -> p (t s)")

        def row_factor():
            m1 = dve.do(lambda: nc.vector.memset(RB[:, 0, :], 1.0))
            m2 = [v_ts(RA[:, t, :], ident[:, :], rs6[:, t:t + 1], None, ALU.mult, None, ready["rs6"]) for t in range(2)]
            yield
            bb = yield from takes(side)
            m3 = p_mm([(bb.ap[:, t * P:(t + 1) * P], RB[:, 0, :], RA[:, t, :], True, True) for t in range(2)],
                      m1, m2, bb.free)
            yield
            m4 = a_copy(R, bb.ap[:, 0:S], m3)
            side.give(bb, m4)
            ready["R"] = m4

        m_uz = [dve.do(lambda: nc.vector.memset(U[:, :, 0:2], 0.0), m_out2)]
        ub = Bufs([U[:, i, :] for i in range(4)])
        cb = Bufs([C[:, i, :] for i in range(3)])
        sg2_free = {}
        sg2_now = {}

        def conv(bank, m, ft, f, gate):
            u = yield from takes(ub)
            cc = yield from takes(cb)
            m0 = a_copy(cc.ap, bank.ap[:, S:512], m, cc.free)
            m1 = v_tt(cc.ap, bank.ap[:, 0:S], cc.ap, ALU.add, m0)
            both.give(bank, m1)
            m1 = v_tt(u.ap[:, 2:258], cc.ap, R, ALU.mult, m1, ready["R"], u.free, m_uz)
            m2 = v_ts(cc.ap, u.ap[:, 0:S], CW[:, 0, ft:ft + 1], None, ALU.mult, None, m1, cc.free)
            yield
            m3 = v_stt(cc.ap, u.ap[:, 1:257], CW[:, 1, ft:ft + 1], cc.ap, ALU.mult, ALU.add, m2)
            m4 = v_stt(cc.ap, u.ap[:, 2:258], CW[:, 2, ft:ft + 1], cc.ap, ALU.mult, ALU.add, m3)
            ub.give(u, m4)
            if gate:
                yield
                m5 = a_fn(ACT.Silu, SG2[:, f, :], cc.ap, m4, sg2_free.get(f))
                cb.give(cc, m5)
                sg2_now[(ft // 4, f)] = m5
                return
            k = ft - FT
            m5 = v_tt(cc.ap, cc.ap, SG2[:, f, :], ALU.mult, m4, sg2_now[(k // 4, f)])
            sg2_free[f] = m5
            yield
            m6 = a_copy(Hh[:, k, :], cc.ap, m5)
            yield
            m7 = v_tt(Hl[:, k, :], cc.ap, r32(Hh[:, k, :]), ALU.subtract, m6)
            cb.give(cc, m7)
            ready[("H2", k)] = [m6, m7]

        both = Bufs([])

        def gemm_t(steps, f0, gate):
            bk = [take_now(both) for _ in range(4)]
            for _, k0, a in steps:
                hi, lo, m_w = chunk()
                for kk in range(a):
                    k = k0 + kk
                    m_l = from_T(k)[2]
                    mms = []
                    for f in range(4):
                        o, fs = bk[f].ap, slice(f * P, (f + 1) * P)
                        mms += [(o, hi[:, kk, fs], TT[:, k, :, :].rearrange("p a s -> p (a s)"), k == 0, False),
                                (o[:, 0:S], lo[:, kk, fs], Th[:, k, :], False, k == KT - 1)]
                    m = p_mm(mms, m_w, m_l, [z.free for z in bk] if k == 0 else None)
                used.append(m)
                if k0 + a == KT:
                    if "R" not in ready:
                        done("R")
                    for f in range(4):
                        spawn(conv(bk[f], m, f0 + f, f, gate), 2 * f)
                if len(side.idle) == 4 and "R" in ready and all(("T", z) in ready for z in range(KT)):
                    both.idle, side.idle = both.idle + side.idle, []
                pump()

        both.idle, main.idle = main.idle, []
        for f in range(NF):
            gemm_t(jff2[f][0], 4 * f, True)
            gemm_t(jff2[f][1], FT + 4 * f, False)
        m_T3 = used[-1]
        main = both

        def from_H2(k):
            m = done(("H2", k))
            return Hh[:, k, :], Hl[:, k, :], m

        ss7, rs7 = stat(8), stat(2)
        mk7 = {}
        gemm(jdown2, FT, 512, from_H2, evac_post(MG2, GB, "g3", ss7, mk7, m_T3), by_half=True)
        bk, mqs = mk7.pop(3)
        m_rs7 = rstd_of(ss7, 4, D, rs7, [v[0] for v in mk7.values()], mqs)
        for t in range(2):
            mk7[(3, t)] = (mqs[t], v_tt(MG2[:, t, 1536:D], bk[t].ap, GB[:, 1536:D], ALU.mult, mqs))
        out_v = A["out"].rearrange("b (t p) d -> p (b t) d", p=P)
        for c in range(4):
            for t in range(2):
                xs = slice(512 * c, 512 * (c + 1))
                m = v_stt(X[:, t, xs], MG2[:, t, xs], rs7[:, t:t + 1], X[:, t, xs], ALU.mult, ALU.add,
                          m_rs7, mk7[(c, t)][1])
                last = sp.dma(out_v[:, t, xs], X[:, t, xs], l_out, m, eng=nc.sync)
        assert at_job["use"] == len(jobs) and not tasks

        for q in (pe, act, dve, pool):
            q.number()
        block = ctx.enter_context(nc.Block())

        @block.sync
        def _(eng):
            sp.emit(eng)
            eng.wait_ge(last.sem, last.value)

        @block.gpsimd
        def _(eng):
            pool.emit(eng)
            eng.wait_ge(ready["lines"].sem, ready["lines"].value)

        @block.scalar
        def _(eng):
            act.emit(eng)

        @block.vector
        def _(eng):
            dve.emit(eng)

        @block.tensor
        def _(eng):
            pe.emit(eng)


def constants():
    f = np.float32
    c = np.zeros((P, 560), f)
    c[:, 0:128] = np.eye(P, dtype=f)
    tri = np.where(np.arange(P)[None, :] <= np.arange(P)[:, None], 0.0, NEG).astype(f)
    c[:, 128:256] = tri
    c[:, 384:512] = tri
    for o, d in ((512, 32), (528, 64)):
        fr = f(500000.0) ** (-np.arange(0, d, 2, dtype=f) / f(d))
        c[:, o:o + d // 2] = fr.astype(f)[None, :]
    b = np.zeros((32, 768), f)
    b[:, 384:768] = NEG
    for i in range(127, 255):
        n = i - 127
        if n < 16:
            k = n
        else:
            k = min(16 + int(f(math.log(n / 16) / math.log(8)) * f(16)), 31)
        b[k, i] = 1.0
        b[:, 384 + i] = 0.0
    return c, b


_INS = ["x", "positions", "attn_norm", "w_in", "q_norm", "w_uq", "kv_norm", "w_ukv", "w_branch_a", "w_branch_b",
        "w_out", "ffn_norm", "w_gate", "w_up", "w_down", "final_norm", "rel_bias_table_2", "norm_g_2",
        "ffn_w_up_2", "ffn_conv_2", "ffn_w_down_2", "swa_w_in_2", "swa_w_out_2", "swa_sinks_2"]


def kernel(**inputs):
    import numpy as _np
    import concourse.bacc as _bacc
    from concourse import mybir as _mybir
    from concourse.bass_utils import run_bass_kernel_spmd as _run

    nc = _bacc.Bacc("TRN2", target_bir_lowering=False, num_devices=1)
    c_main, c_bias = constants()
    arrays = {n: _np.ascontiguousarray(inputs[n]) for n in _INS}
    arrays["c_main"], arrays["c_bias"] = c_main, c_bias
    feed, args = {}, {}
    for name, a in arrays.items():
        feed[f"in_{name}_dram"] = a
        args[name] = nc.dram_tensor(f"in_{name}_dram", a.shape, _mybir.dt.from_np(a.dtype), kind="ExternalInput").ap()
    args["out"] = nc.dram_tensor("out_0_dram", (1, S, D), F32, kind="ExternalOutput").ap()
    build(nc, args)
    r = _run(nc, [feed], core_ids=[0])
    return r.results[0]["out_0_dram"]
```
